# Optimizing a Trainium2 kernel written in Bass

```python
import jax, jax.numpy as jnp
from jax import lax
import numpy as np

D_MODEL = 1024
BATCH = 1
SEQ = 1024
DEPTH = 1

CHUNK = 64
Q_BLOCK = 128
SB_HEADS = 8
SB_HEAD_DIM = 64
SB_WIDTH = SB_HEADS * SB_HEAD_DIM
RW_HEADS = 8
RW_HEAD_DIM = 64
RW_WIDTH = RW_HEADS * RW_HEAD_DIM
W_LORA = 64
A_LORA = 64
G_LORA = 128
GN_EPS = RW_HEAD_DIM * 1e-5
N_BRANCH = 2
SB_COLS = 3 * SB_WIDTH
RW_COLS = 3 * RW_WIDTH + W_LORA + A_LORA + G_LORA
GATE_COLS = N_BRANCH * D_MODEL
IN_COLS = SB_COLS + RW_COLS + GATE_COLS
D_FF = ((8 * D_MODEL + 3 * 256 - 1) // (3 * 256)) * 256
RMS_EPS = 1e-6


def rms_norm(x, g):
    xf = x.astype(jnp.float32)
    y = xf * lax.rsqrt(jnp.mean(xf * xf, axis=-1, keepdims=True) + RMS_EPS)
    return (y * g).astype(x.dtype)

def token_shift(p):
    return jnp.pad(p, ((0, 0), (1, 0), (0, 0)))[:, :-1]

def stick_breaking_attention(q, k, v):
    B, S, H, Dh = q.shape
    scale = Dh ** -0.5
    outs = []
    for i in range(S // Q_BLOCK):
        q0 = i * Q_BLOCK
        kv_len = q0 + Q_BLOCK
        qb = q[:, q0:kv_len]
        kb = k[:, :kv_len]
        vb = v[:, :kv_len]
        z = jnp.einsum('bqhd,bkhd->bhqk', qb, kb).astype(jnp.float32) * scale
        t_idx = q0 + jnp.arange(Q_BLOCK)[:, None]
        s_idx = jnp.arange(kv_len)[None, :]
        strict = s_idx < t_idx
        log_fail = jnp.where(strict, jax.nn.log_sigmoid(-z), 0.0)
        after = lax.cumsum(log_fail, axis=3, reverse=True) - log_fail
        w = jnp.where(strict, jnp.exp(jax.nn.log_sigmoid(z) + after), 0.0)
        outs.append(jnp.einsum('bhqk,bkhd->bqhd', w.astype(vb.dtype), vb))
    return jnp.concatenate(outs, axis=1)

def wkv7_scan(r, decay, k, v, kk, a):
    B, S, H, N = r.shape

    def to_chunks(t):
        return t.astype(jnp.float32).transpose(1, 0, 2, 3).reshape(S // CHUNK, CHUNK, B, H, N)

    def step(state, inp):
        r_t, w_t, k_t, v_t, kk_t, a_t = inp
        sa = jnp.einsum('bhvk,bhk->bhv', state, -kk_t)
        state = (state * w_t[:, :, None, :]
                 + sa[..., None] * (kk_t * a_t)[:, :, None, :]
                 + v_t[..., None] * k_t[:, :, None, :])
        return state, jnp.einsum('bhvk,bhk->bhv', state, r_t)

    def chunk_step(state, chunk_inp):
        return lax.scan(step, state, chunk_inp)

    state0 = jnp.zeros((B, H, N, N), jnp.float32)
    _, y = lax.scan(chunk_step, state0, tuple(to_chunks(t) for t in (r, decay, k, v, kk, a)))
    return y.reshape(S, B, H, N).transpose(1, 0, 2, 3)

def rwkv7_time_mix(p, mu, w0, w_up, a0, a_up, g_up, k_k, k_a, r_k, lnx_w, lnx_b):
    B, S, _ = p.shape
    H, N = RW_HEADS, RW_HEAD_DIM
    p = p + (token_shift(p) - p) * mu
    o1, o2, o3 = RW_WIDTH, 2 * RW_WIDTH, 3 * RW_WIDTH
    r, k, v = p[..., :o1], p[..., o1:o2], p[..., o2:o3]
    xw = p[..., o3:o3 + W_LORA]
    xa = p[..., o3 + W_LORA:o3 + W_LORA + A_LORA]
    xg = p[..., o3 + W_LORA + A_LORA:]
    w_raw = (w0 + jnp.tanh(xw) @ w_up).astype(jnp.float32)
    decay = jnp.exp(-jnp.exp(-jax.nn.softplus(-w_raw) - 0.5))
    a = jax.nn.sigmoid((a0 + xa @ a_up).astype(jnp.float32))
    g = jax.nn.sigmoid(xg) @ g_up
    kk = (k * k_k).astype(jnp.float32).reshape(B, S, H, N)
    kk = kk / jnp.maximum(jnp.linalg.norm(kk, axis=-1, keepdims=True), 1e-12)
    k = k.astype(jnp.float32) * (1.0 + (a - 1.0) * k_a)
    heads = lambda t: t.astype(jnp.float32).reshape(B, S, H, N)
    r_h, k_h, v_h = heads(r), heads(k), heads(v)
    y = wkv7_scan(r_h, heads(decay), k_h, v_h, kk, heads(a))
    mean = jnp.mean(y, axis=-1, keepdims=True)
    var = jnp.mean(jnp.square(y - mean), axis=-1, keepdims=True)
    y = ((y - mean) * lax.rsqrt(var + GN_EPS)).reshape(B, S, RW_WIDTH) * lnx_w + lnx_b
    bonus = (jnp.sum(r_h * k_h * r_k, axis=-1, keepdims=True) * v_h).reshape(B, S, RW_WIDTH)
    return ((y + bonus) * g).astype(p.dtype)

def first_inputs(seed: int = 0) -> dict:
    key = jax.random.key(seed)
    ks = jax.random.split(key, 24)
    L, D = DEPTH, D_MODEL
    nrm = lambda k_, shape, s: jax.random.normal(k_, shape, jnp.float32) * s
    return {
        "x": nrm(ks[0], (BATCH, SEQ, D), 1.0),
        "norm_mix_pre": 1.0 + nrm(ks[1], (L, D), 0.1),
        "w_in": nrm(ks[2], (L, D, IN_COLS), D ** -0.5),
        "b_gate": nrm(ks[3], (L, GATE_COLS), 0.1),
        "mu_rw": jax.random.uniform(ks[4], (L, RW_COLS), jnp.float32),
        "w0": jax.random.uniform(ks[5], (L, RW_WIDTH), jnp.float32, -6.0, 0.0),
        "w_up": nrm(ks[6], (L, W_LORA, RW_WIDTH), 0.1),
        "a0": nrm(ks[7], (L, RW_WIDTH), 0.1),
        "a_up": nrm(ks[8], (L, A_LORA, RW_WIDTH), 0.5 * A_LORA ** -0.5),
        "g_up": nrm(ks[9], (L, G_LORA, RW_WIDTH), G_LORA ** -0.5),
        "k_k": 0.85 + nrm(ks[10], (L, RW_WIDTH), 0.05),
        "k_a": 1.0 + nrm(ks[11], (L, RW_WIDTH), 0.05),
        "r_k": nrm(ks[12], (L, RW_HEADS, RW_HEAD_DIM), 0.1),
        "lnx_w": 1.0 + nrm(ks[13], (L, RW_WIDTH), 0.1),
        "lnx_b": nrm(ks[14], (L, RW_WIDTH), 0.02),
        "w_sb_out": nrm(ks[15], (L, SB_WIDTH, D), SB_WIDTH ** -0.5),
        "w_rw_out": nrm(ks[16], (L, RW_WIDTH, D), RW_WIDTH ** -0.5),
        "w_o": nrm(ks[17], (L, D, D), D ** -0.5),
        "norm_mix_post": 1.0 + nrm(ks[18], (L, D), 0.1),
        "norm_ffn_pre": 1.0 + nrm(ks[19], (L, D), 0.1),
        "w_ffn_gate": nrm(ks[20], (L, D, D_FF), D ** -0.5),
        "w_ffn_up": nrm(ks[21], (L, D, D_FF), D ** -0.5),
        "w_ffn_down": nrm(ks[22], (L, D_FF, D), D_FF ** -0.5),
        "norm_ffn_post": 1.0 + nrm(ks[23], (L, D), 0.1),
    }

def first_block(x, norm_mix_pre, w_in, b_gate, mu_rw, w0, w_up, a0, a_up, g_up, k_k, k_a, r_k,
              lnx_w, lnx_b, w_sb_out, w_rw_out, w_o, norm_mix_post, norm_ffn_pre,
              w_ffn_gate, w_ffn_up, w_ffn_down, norm_ffn_post):
    B, S, D = x.shape
    for l in range(DEPTH):
        h = rms_norm(x, norm_mix_pre[l])
        proj = h @ w_in[l]
        p_sb = proj[..., :SB_COLS]
        p_rw = proj[..., SB_COLS:SB_COLS + RW_COLS]
        gates = jax.nn.sigmoid(proj[..., SB_COLS + RW_COLS:] + b_gate[l])
        q = p_sb[..., :SB_WIDTH].reshape(B, S, SB_HEADS, SB_HEAD_DIM)
        k = p_sb[..., SB_WIDTH:2 * SB_WIDTH].reshape(B, S, SB_HEADS, SB_HEAD_DIM)
        v = p_sb[..., 2 * SB_WIDTH:].reshape(B, S, SB_HEADS, SB_HEAD_DIM)
        o_sb = stick_breaking_attention(q, k, v).reshape(B, S, SB_WIDTH)
        o_rw = rwkv7_time_mix(p_rw, mu_rw[l], w0[l], w_up[l], a0[l], a_up[l], g_up[l],
                              k_k[l], k_a[l], r_k[l], lnx_w[l], lnx_b[l])
        merged = (gates[..., :D] * (o_sb @ w_sb_out[l])
                  + gates[..., D:] * (o_rw @ w_rw_out[l]))
        x = x + rms_norm(merged @ w_o[l], norm_mix_post[l])
        h = rms_norm(x, norm_ffn_pre[l])
        f = (jax.nn.silu(h @ w_ffn_gate[l]) * (h @ w_ffn_up[l])) @ w_ffn_down[l]
        x = x + rms_norm(f, norm_ffn_post[l])
    return x


MIX_WIDTH = D_MODEL
ATT_WIDTH = MIX_WIDTH // 2
GMLP_WIDTH = MIX_WIDTH - ATT_WIDTH
ATT_HEAD_DIM = 64
N_ATT_HEADS = ATT_WIDTH // ATT_HEAD_DIM
N_GMLP_GROUPS = 8
GMLP_GROUP_DIM = GMLP_WIDTH // N_GMLP_GROUPS
CHUNK_2 = 128
D_FF_2 = 2816
CONV_WIDTH = 3
EPS = 1e-6

Q_END = ATT_WIDTH
K_END = 2 * ATT_WIDTH
V_END = 3 * ATT_WIDTH
U_END = V_END + GMLP_WIDTH
G_END = U_END + GMLP_WIDTH
IN_COLS_2 = G_END + N_ATT_HEADS


def rmsnorm(x, gain):
    xf = x.astype(jnp.float32)
    y = xf * lax.rsqrt(jnp.mean(xf * xf, axis=-1, keepdims=True) + EPS)
    return y.astype(x.dtype) * gain

def forgetting_attention(q, k, v, log_f):
    B, S, H, Dh = q.shape
    nb = S // Q_BLOCK
    c = jnp.cumsum(log_f, axis=1)
    c_k = c.transpose(0, 2, 1)[:, :, None, :]
    key_pos = jnp.arange(S)
    qb = q.reshape(B, nb, Q_BLOCK, H, Dh).transpose(1, 0, 2, 3, 4)
    cb = c.reshape(B, nb, Q_BLOCK, H).transpose(1, 0, 3, 2)
    pb = key_pos.reshape(nb, Q_BLOCK)
    scale = Dh ** -0.5

    def block(args):
        qi, ci, pi = args
        logits = jnp.einsum('bqhd,bkhd->bhqk', qi, k).astype(jnp.float32) * scale
        logits = logits + ci[..., None] - c_k
        causal = pi[:, None] >= key_pos[None, :]
        logits = jnp.where(causal, logits, -jnp.inf)
        p = jax.nn.softmax(logits, axis=-1).astype(v.dtype)
        return jnp.einsum('bhqk,bkhd->bqhd', p, v)

    out = lax.map(block, (qb, cb, pb))
    return out.transpose(1, 0, 2, 3, 4).reshape(B, S, H * Dh)

def chunked_spatial_gating(u, vg, v_gain, w_s, b_s):
    B, S, G, Dg = u.shape
    nc = S // CHUNK_2
    vg = rmsnorm(vg, v_gain.reshape(G, Dg))
    vc = vg.reshape(B, nc, CHUNK_2, G, Dg)
    w = w_s * jnp.tril(jnp.ones((CHUNK_2, CHUNK_2), dtype=w_s.dtype))
    mixed = jnp.einsum('gij,bnjgd->bnigd', w, vc) + b_s.T[None, None, :, :, None]
    return (u * mixed.reshape(B, S, G, Dg)).reshape(B, S, G * Dg)

def conv_ffn(x, w_up, conv_w, conv_b, w_down):
    h = x @ w_up
    h = lax.conv_general_dilated(
        h, conv_w[:, None, :], window_strides=(1,),
        padding=[(CONV_WIDTH - 1, 0)],
        dimension_numbers=('NWC', 'WIO', 'NWC'),
        feature_group_count=h.shape[-1]) + conv_b
    a, g = jnp.split(h, 2, axis=-1)
    return (jax.nn.silu(g) * a) @ w_down

def second_inputs(seed: int = 0) -> dict:
    key = jax.random.key(seed)
    ks = jax.random.split(key, 16)
    f32 = jnp.float32
    x = jax.random.normal(ks[0], (BATCH, SEQ, D_MODEL), f32)
    norm_mix_g = 1.0 + 0.02 * jax.random.normal(ks[1], (DEPTH, D_MODEL), f32)
    w_in = jax.random.normal(ks[2], (DEPTH, D_MODEL, IN_COLS_2), f32) * D_MODEL ** -0.5
    b_forget = 2.0 + 0.5 * jax.random.normal(ks[3], (DEPTH, N_ATT_HEADS), f32)
    gmlp_norm_g = 1.0 + 0.02 * jax.random.normal(ks[4], (DEPTH, GMLP_WIDTH), f32)
    w_spatial = jax.random.normal(ks[5], (DEPTH, N_GMLP_GROUPS, CHUNK_2, CHUNK_2), f32) * CHUNK_2 ** -0.5
    b_spatial = 1.0 + 0.1 * jax.random.normal(ks[6], (DEPTH, N_GMLP_GROUPS, CHUNK_2), f32)
    w_out = jax.random.normal(ks[7], (DEPTH, MIX_WIDTH, D_MODEL), f32) * MIX_WIDTH ** -0.5
    norm_ffn_g = 1.0 + 0.02 * jax.random.normal(ks[8], (DEPTH, D_MODEL), f32)
    w_up = jax.random.normal(ks[9], (DEPTH, D_MODEL, 2 * D_FF_2), f32) * D_MODEL ** -0.5
    conv_w = jax.random.normal(ks[10], (DEPTH, CONV_WIDTH, 2 * D_FF_2), f32) * CONV_WIDTH ** -0.5
    conv_b = 0.01 * jax.random.normal(ks[11], (DEPTH, 2 * D_FF_2), f32)
    w_down = jax.random.normal(ks[12], (DEPTH, D_FF_2, D_MODEL), f32) * D_FF_2 ** -0.5
    norm_final_g = 1.0 + 0.02 * jax.random.normal(ks[13], (D_MODEL,), f32)
    return {"x": x, "norm_mix_g": norm_mix_g, "w_in": w_in, "b_forget": b_forget,
            "gmlp_norm_g": gmlp_norm_g, "w_spatial": w_spatial, "b_spatial": b_spatial,
            "w_out": w_out, "norm_ffn_g": norm_ffn_g, "w_up": w_up, "conv_w": conv_w,
            "conv_b": conv_b, "w_down": w_down, "norm_final_g": norm_final_g}

def second_block(x, norm_mix_g, w_in, b_forget, gmlp_norm_g, w_spatial, b_spatial,
              w_out, norm_ffn_g, w_up, conv_w, conv_b, w_down, norm_final_g):
    B, S, _ = x.shape
    h = x
    for layer in range(DEPTH):
        xn = rmsnorm(h, norm_mix_g[layer])
        proj = xn @ w_in[layer]
        q = proj[..., :Q_END].reshape(B, S, N_ATT_HEADS, ATT_HEAD_DIM)
        k = proj[..., Q_END:K_END].reshape(B, S, N_ATT_HEADS, ATT_HEAD_DIM)
        v = proj[..., K_END:V_END].reshape(B, S, N_ATT_HEADS, ATT_HEAD_DIM)
        log_f = jax.nn.log_sigmoid(
            (proj[..., G_END:] + b_forget[layer]).astype(jnp.float32))
        att = forgetting_attention(q, k, v, log_f)
        uv = jax.nn.gelu(proj[..., V_END:G_END])
        u = uv[..., :GMLP_WIDTH].reshape(B, S, N_GMLP_GROUPS, GMLP_GROUP_DIM)
        vg = uv[..., GMLP_WIDTH:].reshape(B, S, N_GMLP_GROUPS, GMLP_GROUP_DIM)
        sg = chunked_spatial_gating(u, vg, gmlp_norm_g[layer], w_spatial[layer], b_spatial[layer])
        mix = jnp.concatenate([att, sg], axis=-1)
        h = h + mix @ w_out[layer]
        h = h + conv_ffn(rmsnorm(h, norm_ffn_g[layer]), w_up[layer], conv_w[layer],
                         conv_b[layer], w_down[layer])
    return rmsnorm(h, norm_final_g)


def setup_inputs(seed=0):
    out = dict(first_inputs(seed))
    for name, value in second_inputs(seed + 1).items():
        if name != "x":
            out[name + "_2"] = value
    return out


def reference(
    x, norm_mix_pre, w_in, b_gate, mu_rw, w0, w_up, a0, a_up, g_up, k_k, k_a, r_k, lnx_w, lnx_b,
    w_sb_out, w_rw_out, w_o, norm_mix_post, norm_ffn_pre, w_ffn_gate, w_ffn_up, w_ffn_down,
    norm_ffn_post, norm_mix_g_2, w_in_2, b_forget_2, gmlp_norm_g_2, w_spatial_2, b_spatial_2,
    w_out_2, norm_ffn_g_2, w_up_2, conv_w_2, conv_b_2, w_down_2, norm_final_g_2,
):
    x = first_block(
        x, norm_mix_pre, w_in, b_gate, mu_rw, w0, w_up, a0, a_up, g_up, k_k, k_a, r_k, lnx_w,
        lnx_b, w_sb_out, w_rw_out, w_o, norm_mix_post, norm_ffn_pre, w_ffn_gate, w_ffn_up,
        w_ffn_down, norm_ffn_post,
    )
    return second_block(
        x, norm_mix_g_2, w_in_2, b_forget_2, gmlp_norm_g_2, w_spatial_2, b_spatial_2, w_out_2,
        norm_ffn_g_2, w_up_2, conv_w_2, conv_b_2, w_down_2, norm_final_g_2,
    )


_drawn_inputs = setup_inputs


def setup_inputs(seed=0):
    import zlib

    import numpy as np

    out = dict(_drawn_inputs(seed))
    spreads = {}
    factors = {'lnx_b': 5.214,
     'norm_mix_g_2': 5.91,
     'gmlp_norm_g_2': 8.0,
     'norm_ffn_g_2': 5.913,
     'conv_b_2': 28.655,
     'norm_final_g_2': 7.723}
    for name, (base, spread) in spreads.items():
        noise = np.random.default_rng([zlib.crc32(name.encode()), seed]).standard_normal(out[name].shape)
        drawn = base * np.exp(spread * noise) if base else spread * noise
        out[name] = __import__('jax').numpy.asarray(drawn.astype(out[name].dtype))
    for name, factor in factors.items():
        out[name] = (out[name] * factor).astype(out[name].dtype)
    return out
```

```python
from contextlib import ExitStack

import concourse.bass as bass
import numpy as np
from concourse import mybir

F32 = mybir.dt.float32
F32R = mybir.dt.float32r
BF16 = mybir.dt.bfloat16
ALU = mybir.AluOpType
ACT = mybir.ActivationFunctionType
AX_X = mybir.AxisListType.X

P = 128
S = 1024
D = 1024
KT = D // P
NB = S // P
HALF = 512
HD = 64
NPAIR = 4
CH = 64
NCH = S // CH
SB_W = 512
RW_COL0 = 3 * SB_W
GATE_COL0 = RW_COL0 + 3 * SB_W + 256
DFF = 2816
FT = DFF // P
NG = FT // 2
RMS_EPS = 1e-6
GN_EPS = HD * 1e-5
KK_FLOOR = 1e-12
DECAY = float(np.exp(-0.5))

PV = 10
C_PAIR = 0
C_MU2 = C_PAIR + NPAIR * PV
C_GPRE = C_MU2 + 2
C_BGATE = C_GPRE + KT
C_FPRE = C_BGATE + 2 * KT
C_GPRE2 = C_FPRE + KT
C_FPRE2 = C_GPRE2 + KT
C_VG = C_FPRE2 + KT
N_VEC = C_VG + 4
C_CONV = N_VEC
N_COL = C_CONV + FT * 8


def build(nc, a, out):
    ctx = ExitStack()
    with ctx:
        sem_of = {}

        def sem(name):
            if name not in sem_of:
                sem_of[name] = ctx.enter_context(nc.semaphore(name))
            return sem_of[name]

        def sb(name, shape, dt=F32, scope=ctx):
            return scope.enter_context(nc.sbuf_tensor(name, shape, dt))

        x_tok = a["x"][0].rearrange("(b p) d -> p b d", p=P)
        out_tok = out[0].rearrange("(b p) d -> p b d", p=P)
        kmaj = lambda w: w[0].rearrange("(k p) c -> p k c", p=P)
        w_in, w_in2 = kmaj(a["w_in"]), kmaj(a["w_in_2"])
        w_sb, w_rw, w_o = kmaj(a["w_sb_out"]), kmaj(a["w_rw_out"]), kmaj(a["w_o"])
        w_g, w_u, w_d = kmaj(a["w_ffn_gate"]), kmaj(a["w_ffn_up"]), kmaj(a["w_ffn_down"])
        w_out2, w_up2, w_down2 = kmaj(a["w_out_2"]), kmaj(a["w_up_2"]), kmaj(a["w_down_2"])
        o_scr = nc.dram_tensor("o_scratch", [8, P, S], F32, kind="Internal").ap()
        x1_scr = nc.dram_tensor("x1_scratch", [P, NB, D], F32, kind="Internal").ap()
        x3_scr = nc.dram_tensor("x3_scratch", [P, NB, D], F32, kind="Internal").ap()
        x2_scr = nc.dram_tensor("x2_scratch", [P, NB, D], F32, kind="Internal").ap()

        PS = ctx.enter_context(nc.psum_tensor("PS", [P, 8, HALF], F32))
        hH, hL = sb("hH", [P, KT, S], F32R), sb("hL", [P, KT, S], F32R)
        raw = [sb(f"w_raw{s}", [P, KT, P]) for s in range(2)]
        wH = [sb(f"w_H{s}", [P, KT, P], F32R) for s in range(2)]
        wL = [sb(f"w_L{s}", [P, KT, P], F32R) for s in range(2)]
        ident = sb("ident", [P, P])
        cols = sb("cols", [P, N_COL])
        pg = sb("gate_bias", [P, 4])
        eps = sb("eps", [P, 2])
        ss, sd, rstd, ss2, sd2, rstd2 = (sb(n, [P, NB]) for n in (
            "sum_squares", "std", "rstd", "sum_squares2", "std2", "rstd2"))
        with ExitStack() as scope:
            rows = sb("vector_rows", [P, 3, P], scope=scope)
            xb = sb("x_blocks", [P, NB, D], scope=scope)
            junk = sb("squares", [P, D], scope=scope)
            HG = [sb("h_gained", [P, KT, P], scope=scope)]
        with ExitStack() as scope:
            T = lambda n, shape=(P, S), dt=F32: sb(n, list(shape), dt, scope)
            mask_upper, mask_incl = T("mask_upper", (P, P)), T("mask_incl", (P, P))
            mask_lvl = T("mask_level", (P, 6, P))
            same_head = T("same_head", (P, P))
            mask_att = T("mask_att", (P, P))
            bar_att = T("bar_att", (P, P), BF16)
            neg_tri, neg_one = T("neg_tri", (P, P)), T("neg_one", (P, P))
            ident_b = T("ident_bf16", (P, P), BF16)
            chunk_keep = T("chunk_keep", (P, S), BF16)
            lora, pv = T("lora", (P, 2, P)), T("pair_vectors", (P, PV))
            lx, sg = T("tanh_xw_xa"), T("sigmoid_xg")
            xs, dt = T("shift_source", (P, S + 1)), T("dve_work")
            r_, k_, v_ = T("r_mixed"), T("k_mixed"), T("v_mixed")
            a_, lsum, enl = T("a_gate"), T("log_decay_sum"), T("exp_minus_l")
            elx = T("exp_l", (P, NCH, CH + 1))
            kk = T("kk")
            rt, at_, bt, kt_ = T("r_dec"), T("minus_kk_dec"), T("b_inc"), T("k_inc")
            sq, bv, gg, yt, sa, ut, zt = rt, r_, lsum, xs[:, 1:S + 1], a_, kk, enl
            with ExitStack() as scope_att:
                T = lambda n, shape=(P, S), dt=F32: sb(n, list(shape), dt, scope_att)
                qf, kf, vf, vt, ot = T("q_att"), T("k_att"), T("v_att"), T("v_tok"), T("o_att")
                na, sp_, wt, ssum = ([T(f"{n}{i}", (P, HALF)) for i in range(2)]
                                     for n in ("ln_term", "softplus_z", "weights", "softplus_later"))
            with ExitStack() as scope_rw:
                T = lambda n, shape=(P, HALF), dt=F32: sb(n, list(shape), dt, scope_rw)
                tokA, tokB, tokK, tokV = (T(n, (P, NB, P)) for n in ("a_tok", "b_tok", "k_tok", "v_tok_rw"))
                nab, nak, tm, tmT, qm = ([T(f"{n}{h}", (P, 4, P)) for h in range(2)]
                                         for n in ("n_ab", "n_ak", "inv", "inv_t", "level"))
                mv = [T(f"m_ak_v{h}", (P, 4, HD)) for h in range(2)]
                nr = [[T(f"n_r{i}{h}", (P, 2, P)) for h in range(2)] for i in range(2)]
                ss_ = [T(f"state{i}", (P, P)) for i in range(2)]


        f32 = lambda t: t.bitcast(F32)

        def at(c, it=None, per=0):
            return c if it is None else it * per + c

        NA_ = 2 * sum(4 * qh + 4 for qh in range(2))
        SHARED = {}
        for names, phases, count in (
                ("block_normalised", "ADEGH", NB), ("block_transposed block_gained block_H block_L", "ADEG", NB),
                ("y_done", "DG", 6), ("y_copied", "DG", NB), ("squares std rstd", "ADE", NB), ("y_gained", "DE", NB),
                ("gain_loaded", "DEH", 16), ("x_loaded0 x_loaded1", "DEGH", 8 * NB), ("x_new", "DEGH", NB),
                ("x_stored0 x_stored1", "DEG", 8 * NB), ("squares2 std2 rstd2", "DEGH", NB),
                ("down_loaded", "EH", 16 * NG), ("down_H down_L", "EH", NG),
                ("silu hidden hidden_H hidden_L", "EH", 2 * NG), ("y_part", "EH", 8 * NG),
                ("y_added", "EH", 8 * NG + NB)):
            for name in names.split():
                SHARED[name] = {phase: count for phase in phases}
        for name, count in (("qk_product", 4 * NA_), ("weights_used", 4 * NA_), ("weights_written", 4 * NA_),
                            ("v_att_turned", 4), ("norm_sums", 4), ("v_att_tok", 4), ("norm_root", 4),
                            ("norm_squares", 4), ("dense_tile_taken", 2 + 6 * NPAIR), ("pair_vectors_set", 4),
                            ("masks_written", 1)):
            SHARED[name] = {"B": count, "F": 0}

        def since(phase, name, value):
            before = sum(n for ph, n in SHARED[name].items() if ph < phase)
            return value + before if before else value

        class Chain:

            def __init__(self, eng, s, it=None, per=0, base=0, value=None):
                self.eng, self.s, self.it, self.per, self.n = eng, s, it, per, 0
                self.value = value or (lambda n: at(base + n, it, per))

            def __call__(self, ins):
                self.n += 1
                ins.then_inc(self.s, 1)
                self.eng.wait_ge(self.s, self.value(self.n))

            def end(self):
                assert self.it is None or self.n == self.per, (self.n, self.per)

        with ExitStack() as scope:
            T = lambda n, shape=(P, S), dt=F32: sb(n, list(shape), dt, scope)
            oH, oL = T("o_H", (P, KT, S), F32R), T("o_L", (P, KT, S), F32R)
            mg = T("merged", (P, KT, S))
            g_sb, g_rw = T("gate_sb"), T("gate_rw")
        with ExitStack() as scope:
            T = lambda n, shape=(P, S), dt=F32: sb(n, list(shape), dt, scope)
            xD = [T(f"x_res{i}") for i in range(2)]
            x1D = [T(f"x_new{i}") for i in range(2)]
            hnD, HG2, gBD, junkD = T("h_normalised", (P, NB, D)), T("h_gained2", (P, KT, P)), T("gain_rows"), T("junk_d")
            for_D = (None, xD, x1D, hnD, HG2, gBD, junkD[:, :])
        with ExitStack() as scope:
            T = lambda n, shape=(P, S), dt=F32: sb(n, list(shape), dt, scope)
            yacc = T("ffn_sum", (P, NB, D))
            rawD = T("down_raw", (P, 2, D))
            dH, dL = T("down_H", (P, 2, D), F32R), T("down_L", (P, 2, D), F32R)
            hdH, hdL = T("hidden_H", (P, 2, S), F32R), T("hidden_L", (P, 2, S), F32R)
            hf, sil, cvo = T("hidden"), T("silu_out"), T("conv_out")
            cvt = T("conv_columns", (P, 16))
            xE = [T(f"x_res_e{i}") for i in range(2)]
            x1E = [T(f"x_new_e{i}") for i in range(2)]
            HG3, gBE, junkE = T("h_gained3", (P, KT, P)), T("gain_rows_e"), T("junk_e")
            for_E = (None, xE, x1E, yacc, HG3, gBE, junkE[:, :])
        with ExitStack() as scope:
            T = lambda n, shape=(P, S), dt=F32: sb(n, list(shape), dt, scope)
            mixH, mixL = T("mix_H", (P, KT, S), F32R), T("mix_L", (P, KT, S), F32R)
            with ExitStack() as s1:
                T = lambda n, shape=(P, S), dt=F32: sb(n, list(shape), dt, s1)
                same_F, keep_F = T("same_group", (P, P)), T("keep_spatial", (P, P))
                bar_F, ident_F = T("bar_f", (P, P), BF16), T("ident_bf16_f", (P, P), BF16)
                tiles_F = [T(n) for n in ("q_f", "k_f", "u_gate", "vg_gate", "v_tok_f", "p_turned0", "p_turned1")]
                q_F, k_F, u_F, vg_F, vt_F = [t[:, :] for t in tiles_F[:5]]
                vt_F, pT = tiles_F[4], tiles_F[5:7]
                v_F = pT[0][:, :]
                lg = [T(f"logits{i}") for i in range(2)]
                c_keys = [T(f"c_keys{i}") for i in range(2)]
                f_log, f_abs, c_row = lg[0][0:8, :], lg[1][0:8, :], pT[1][0:8, :]
                b_fg = T("forget_bias", (8, 1))
                c_cols, c_q = T("c_columns", (P, NB, 8)), T("c_queries", (P, NB, 2))
                vg_gain, nmax, den = T("vg_gain", (P, 1)), T("minus_max", (P, 16)), T("denominator", (P, 16))
                wsp, wspT, bsp = T("w_spatial", (P, 2, P)), T("w_spatial_t", (P, 2, P)), T("b_spatial", (P, P))
            with ExitStack() as s1:
                T = lambda n, shape=(P, S), dt=F32: sb(n, list(shape), dt, s1)
                xG = [T(f"x_res_g{i}") for i in range(2)]
                x1G = [T(f"x_new_g{i}") for i in range(2)]
                hnG, HG4 = T("h_normalised_g", (P, NB, D)), T("h_gained4", (P, KT, P))
                for_G = (None, xG, x1G, hnG, HG4, None, HG4[:, :, :].rearrange("p k t -> p (k t)"))

        den_col = lambda s: 2 * (s % NB) + s // NB

        s_raw = [sem(f"w_raw_loaded{s}") for s in range(2)]
        s_wH, s_wL, s_used = sem("w_H_written"), sem("w_L_written"), sem("w_unit_used")

        s_held = sem("sp_load_held")

        def load_unit(e, c, src, it=None, per=0, dst=None):
            if c >= 2:
                e.wait_ge(s_wH, at(c - 1, it, per))
                e.wait_ge(s_wL, at(c - 1, it, per))
                e.sem_inc(s_held, 1)
            e.dma_start(raw[c % 2][:, :, :] if dst is None else dst, src).then_inc(s_raw[c % 2], 16)

        def split_H(e, c, it=None, per=0):
            e.wait_ge(s_raw[c % 2], at(16 * (c // 2 + 1), it, 8 * per))
            if c >= 2:
                e.wait_ge(s_used, at(c - 1, it, per))
            e.activation(wH[c % 2][:, :, :], raw[c % 2][:, :, :], ACT.Copy).then_inc(s_wH, 1)

        def split_L(e, c, it=None, per=0):
            e.wait_ge(s_wH, at(c + 1, it, per))
            e.tensor_tensor(wL[c % 2][:, :, :], raw[c % 2][:, :, :], f32(wH[c % 2][:, :, :]),
                            ALU.subtract).then_inc(s_wL, 1)

        def bank2(b):
            return PS[:, b:b + 2, :].rearrange("p a n -> p (a n)")

        def dense(e, c, bank, it=None, per=0, ks=range(KT), xH=hH, xL=hL, x0=0, last=True):
            e.wait_ge(s_wL, at(c + 1, it, per))
            w_h, w_l = wH[c % 2], wL[c % 2]
            for i, k in enumerate(ks):
                passes = [(w_h, xH), (w_h, xL), (w_l, xH)]
                for j, (w, x) in enumerate(passes):
                    for half in range(2):
                        mm = e.matmul(PS[:, bank + half, :], w[:, k, :],
                                      x[:, k - x0, half * HALF:(half + 1) * HALF],
                                      start=(i == 0 and j == 0), stop=(i == len(ks) - 1 and j == 2))
            if last:
                mm.then_inc(s_used, 1)
            return mm

        def dense_piece(e, c, bank, k, half, it, per):
            if k == 0 and half == 0:
                e.wait_ge(s_wL, at(c + 1, it, per))
            w_h, w_l = wH[c % 2], wL[c % 2]
            for j, (w, x) in enumerate([(w_h, hH), (w_h, hL), (w_l, hH)]):
                mm = e.matmul(PS[:, bank + half, :], w[:, k, :], x[:, k, half * HALF:(half + 1) * HALF],
                              start=(k == 0 and j == 0), stop=(k == KT - 1 and j == 2))
            if k == KT - 1 and half == 1:
                mm.then_inc(s_used, 1)

        def dense_rows(e, w_h, w_l, k, bank, tok, first, last, xH=hH, xL=hL):
            passes = [(xH, w_h), (xL, w_h), (xH, w_l)]
            for j, (x, w) in enumerate(passes):
                for half in range(2):
                    mm = e.matmul(PS[:, bank + half, :], x[:, k, tok * P:(tok + 1) * P],
                                  w[:, half * HALF:(half + 1) * HALF],
                                  start=(first and j == 0), stop=(last and j == 2))
            return mm

        s_rows, s_cols = sem("vector_rows_loaded"), sem("vector_columns_written")
        s_identz, s_ident, s_colsT = sem("identity_zeroed"), sem("identity_written"), sem("columns_transposed")

        def vector_rows():
            v = lambda n: a[n][0].rearrange("(k p) -> k p", p=P)
            mu = v("mu_rw")
            got = [(0, C_PAIR + i, PV, NPAIR, r) for i, r in enumerate(
                [mu[0:4], mu[4:8], mu[8:12], v("w0"), v("a0"), v("k_k"), v("k_a"),
                 a["r_k"][0].rearrange("(k h) n -> k (h n)", h=2), v("lnx_w"), v("lnx_b")])]
            got += [(0, C_MU2, 1, 2, mu[12:14]), (0, C_GPRE, 1, KT, v("norm_mix_pre")),
                    (0, C_BGATE, 1, 2 * KT, v("b_gate")), (0, C_FPRE, 1, KT, v("norm_ffn_pre")),
                    (0, C_GPRE2, 1, KT, v("norm_mix_g_2")), (0, C_FPRE2, 1, KT, v("norm_ffn_g_2")),
                    (0, C_VG, 1, 4, v("gmlp_norm_g_2"))]
            cw = a["conv_w_2"][0].rearrange("w (t p) -> w t p", p=P)
            cb = v("conv_b_2")
            for part in range(2):
                for i in range(4):
                    src = cw[i] if i < 3 else cb
                    for h in range(2):
                        t0 = part * FT + h * (FT // 2)
                        got.append((1 + h, 4 * part + i, 8, FT // 2, src[t0:t0 + FT // 2]))
            return got

        ROWS = vector_rows()
        N_ROWS = [N_VEC, 4 * FT, 4 * FT]


        def turn_bank(tag, c):
            return (2 if tag == "E" else 4) * (c % 2)

        def to_feature_pe(e, tag, hn, b, c, it=None, per=0):
            e.wait_ge(sem("block_normalised"), since(tag, "block_normalised", at(c + 1, it, per)))
            if c >= 2:
                e.wait_ge(sem("block_gained"), since(tag, "block_gained", at(c - 1, it, per)))
            for k in range(KT):
                mm = e.transpose(PS[:, turn_bank(tag, c) + k // 4, (k % 4) * P:(k % 4 + 1) * P],
                                 hn[:, k * P:(k + 1) * P], ident[:, :])
            mm.then_inc(sem("block_transposed"), 1)

        def to_feature_gain(e, tag, c, gcol, gained=None, it=None, per=0):
            e.wait_ge(sem("block_transposed"), since(tag, "block_transposed", at(c + 1, it, per)))
            if c >= 1:
                e.wait_ge(sem("block_L"), since(tag, "block_L", at(c, it, per)))
            gained = HG[0] if gained is None else gained
            e.tensor_tensor(gained[:, :, :], bank2(turn_bank(tag, c)).rearrange("p (k t) -> p k t", t=P),
                            cols[:, gcol:gcol + KT].rearrange("p (k o) -> p k o", o=1).to_broadcast([P, KT, P]),
                            ALU.mult).then_inc(sem("block_gained"), 1)

        def to_feature_H(e, tag, c, dst, gained=None, it=None, per=0):
            gained = HG[0] if gained is None else gained
            e.wait_ge(sem("block_gained"), since(tag, "block_gained", at(c + 1, it, per)))
            if c >= 1:
                e.wait_ge(sem("block_L"), since(tag, "block_L", at(c, it, per)))
            e.activation(hH[:, :, dst], gained[:, :, :], ACT.Copy).then_inc(sem("block_H"), 1)

        def to_feature_L(e, tag, c, dst, gained=None, it=None, per=0):
            gained = HG[0] if gained is None else gained
            e.wait_ge(sem("block_H"), since(tag, "block_H", at(c + 1, it, per)))
            e.tensor_tensor(hL[:, :, dst], gained[:, :, :], f32(hH[:, :, dst]), ALU.subtract)\
                .then_inc(sem("block_L"), 1)

        s_x = [sem(f"x_blocks{i}_loaded") for i in range(NB // 2)]
        s_ss, s_sd, s_rs = sem("squares"), sem("std"), sem("rstd")
        s_eps = sem("constants_set")

        def sp_A(e):
            for i in range(NB // 2):
                e.dma_start(xb[:, 2 * i:2 * i + 2, :], x_tok[:, 2 * i:2 * i + 2, :]).then_inc(s_x[i], 16)

        def act_A(e):
            e.wait_ge(s_eps, 2)
            for b in range(NB):
                e.wait_ge(s_x[b // 2], 16)
                if b:
                    e.wait_ge(s_ss, b)
                e.activation(junk[:, :], xb[:, b, :], ACT.Square, accum_out=ss[:, b:b + 1]).then_inc(s_ss, 1)
                e.wait_ge(s_ss, b + 1)
                e.activation(sd[:, b:b + 1], ss[:, b:b + 1], ACT.Sqrt, scale=1.0 / D,
                             bias=eps[:, 0:1]).then_inc(s_sd, 1)
                if b >= 2:
                    to_feature_H(e, "A", b - 2, slice((b - 2) * P, (b - 1) * P))
            for b in range(NB - 2, NB):
                to_feature_H(e, "A", b, slice(b * P, (b + 1) * P))

        def dve_A(e):
            e.memset(eps[:, 0:1], RMS_EPS).then_inc(s_eps, 1)
            e.memset(eps[:, 1:2], GN_EPS).then_inc(s_eps, 1)
            for t in range(3):
                e.wait_ge(s_colsT, t + 1)
                c0 = [0, C_CONV, C_CONV + 4 * FT][t]
                e.tensor_copy(cols[:, c0:c0 + N_ROWS[t]], PS[:, 2 + t, 0:N_ROWS[t]]).then_inc(s_cols, 1)
            e.wait_ge(s_cols, 3)
            for b in range(NB):
                e.wait_ge(s_sd, b + 1)
                e.reciprocal(rstd[:, b:b + 1], sd[:, b:b + 1]).then_inc(s_rs, 1)
                e.wait_ge(s_rs, b + 1)
                e.tensor_scalar(xb[:, b, :], xb[:, b, :], rstd[:, b:b + 1], None, ALU.mult)\
                    .then_inc(sem("block_normalised"), 1)
                if b:
                    to_feature_gain(e, "A", b - 1, C_GPRE)
                    to_feature_L(e, "A", b - 1, slice((b - 1) * P, b * P))
            to_feature_gain(e, "A", NB - 1, C_GPRE)
            to_feature_L(e, "A", NB - 1, slice((NB - 1) * P, NB * P))

        def pool_A(e):
            e.memset(ident[:, :], 0.0).then_inc(s_identz, 1)
            e.wait_ge(s_identz, 1)
            e.affine_select(out=ident[:, :], in_=ident[:, :], compare_op=ALU.not_equal, fill=1.0,
                            base=0, pattern=[[-1, P]], channel_multiplier=1).then_inc(s_ident, 1)

        def act_dma_A(e):
            for t, r0, step, n, src in ROWS:
                e.dma_start(rows[r0:r0 + (n - 1) * step + 1:step, t, :], src).then_inc(s_rows, 16)

        def pe_A(e):
            e.wait_ge(s_ident, 1)
            e.wait_ge(s_rows, 16 * len(ROWS))
            for t in range(3):
                n = N_ROWS[t]
                e.transpose(PS[:, 2 + t, 0:n], rows[0:n, t, :], ident[0:n, 0:n]).then_inc(s_colsT, 1)
            for b in range(NB):
                if b == 0:
                    e.wait_ge(s_cols, 3)
                to_feature_pe(e, "A", xb[:, b, :], b, b)

        UPB = 6
        tile_bank = (4, 6, 2, 6, 2, 6)
        s_pv = sem("pair_vectors_set")
        s_evac = sem("dense_tile_taken")
        s_lxv = sem("lora_inputs_mixed")
        s_masks, s_lora = sem("masks_written"), sem("lora_loaded")
        N_MASK_STEPS = 48

        ATT = [(h, qh, kb) for h in range(2) for qh in range(2) for kb in range(4 * qh + 3, -1, -1)]
        NA = len(ATT)
        ND = sum(kb >= 4 * qh for _, qh, kb in ATT)
        NS_ = NA - 4
        q_lo = lambda qh, kb: max(kb * P - qh * HALF, 0)
        diag_no = [sum(kb >= 4 * qh for _, qh, kb in ATT[:s + 1]) for s in range(NA)]
        sum_no = [sum(kb > 0 for _, qh, kb in ATT[:s + 1]) for s in range(NA)]
        z_bank = lambda s: 4 + s % 3
        o_bank = lambda g: (7, 3)[g % 2]

        def unit_cols_B(p):
            return [RW_COL0 + 4 * P * i + p * P for i in range(3)] + [4 * P * i + p * P for i in range(3)]

        def sp_B(e):
            for i in range(3):
                c0 = [RW_COL0 + 3 * SB_W, RW_COL0 + 3 * SB_W + P, RW_COL0][i]
                load_unit(e, i, w_in[:, :, c0:c0 + P])
            with e.Fori(0, NPAIR) as p:
                for i in range(1, UPB + 1):
                    c0 = [RW_COL0 + 512, RW_COL0 + 1024, 0, 512, 1024, RW_COL0 + P][i - 1]
                    load_unit(e, 2 + i, w_in[:, :, bass.ds(p * P + c0, P)], p, UPB)

        def pool_masks(e):
            e.wait_ge(sem("block_L"), since("A", "block_L", NB))
            s = sem("mask_steps")
            ch = Chain(e, s)

            def keep(t, op, base, pattern, cm, fill=0.0):
                return e.affine_select(out=t, in_=t, compare_op=op, fill=fill, base=base,
                                       pattern=pattern, channel_multiplier=cm)

            ch(e.memset(same_head[:, :], 0.0))
            ch(e.memset(same_head[0:64, 0:64], 1.0))
            ch(e.memset(same_head[64:P, 64:P], 1.0))
            ch(e.tensor_copy(mask_upper[:, :], same_head[:, :]))
            ch(e.tensor_copy(mask_incl[:, :], same_head[:, :]))
            ch(keep(mask_upper[:, :], ALU.is_gt, 0, [[1, P]], -1))
            ch(keep(mask_incl[:, :], ALU.is_ge, 0, [[1, P]], -1))
            for l in range(6):
                w = 2 << l
                v = mask_lvl[:, l, :].rearrange("p (g w) -> p g w", w=w)
                sub = v[:, :, 0:w // 2]
                ch(e.memset(mask_lvl[:, l, :], 0.0))
                ch(e.memset(sub, 1.0))
                ch(keep(sub, ALU.is_ge, -w // 2, [[-w, P // w], [0, w // 2]], 1))
                ch(keep(sub, ALU.is_ge, w - 1, [[w, P // w], [0, w // 2]], -1))
                ch(keep(mask_lvl[:, l, :], ALU.not_equal, 0, [[-1, P]], 1, fill=1.0))
            ch(e.memset(neg_one[:, :], -1.0))
            ch(e.memset(neg_tri[:, :], -1.0))
            ch(keep(neg_tri[:, :], ALU.is_ge, 0, [[-1, P]], 1))
            ch(e.memset(mask_att[:, :], 1.0))
            ch(keep(mask_att[:, :], ALU.is_gt, 0, [[1, P]], -1))
            ch(e.memset(bar_att[:, :], 0.0))
            ch(keep(bar_att[:, :], ALU.is_gt, 0, [[1, P]], -1, fill=-1e30))
            ch(e.tensor_copy(ident_b[:, :], ident[:, :]))
            ch(e.memset(chunk_keep[:, :], 1.0))
            ch(e.memset(chunk_keep[:, :].rearrange("p (c t) -> p c t", t=CH)[:, :, 0:1], 0.0))
            ch(e.memset(elx[:, :, 0:1], 1.0))
            e.memset(xs[:, 0:1], 0.0).then_inc(s_masks, 1)
            assert ch.n == N_MASK_STEPS, ch.n

        def pool_B(e):
            with e.Fori(0, NPAIR) as p:
                def softplus_part(s):
                    h, qh, kb = ATT[s]
                    lo = q_lo(qh, kb)
                    t = sp_[s % 2]
                    e.wait_ge(sem("softplus_written"), at(s + 1, p, NA))
                    if kb >= 4 * qh:
                        e.tensor_tensor(t[:, lo:lo + P], t[:, lo:lo + P], mask_att[:, :], ALU.mult)\
                            .then_inc(sem("softplus_masked"), 1)
                        e.wait_ge(sem("softplus_masked"), at(diag_no[s], p, ND))
                    if kb > 0:
                        first = kb == 4 * qh + 3
                        new, old = ssum[s % 2], ssum[(s + 1) % 2]
                        plo = HALF if first else q_lo(qh, kb + 1)
                        if s >= 1:
                            e.wait_ge(sem("exponent_summed"), at(s, p, NA))
                        ins = None
                        if plo < HALF:
                            e.wait_ge(sem("softplus_summed"), at(sum_no[s - 1], p, NS_))
                            ins = e.tensor_tensor(new[:, plo:HALF], old[:, plo:HALF], t[:, plo:HALF], ALU.add)
                        if lo < plo:
                            ins = e.tensor_tensor(new[:, lo:plo], t[:, lo:plo], mask_att[:, :], ALU.mult)
                        ins.then_inc(sem("softplus_summed"), 1)

                for s in range(NA):
                    softplus_part(s)
                e.wait_ge(sem("o_att_taken"), 4 * p + 4)
                e.dma_start(o_scr[bass.ds(p, 1), :, :].rearrange("o p t -> (o p) t"), ot[:, :])\
                    .then_inc(sem("o_att_stored"), 16)
                e.wait_ge(sem("o_rw_written"), p + 1)
                e.dma_start(o_scr[bass.ds(p + NPAIR, 1), :, :].rearrange("o p t -> (o p) t"), dt[:, :])\
                    .then_inc(sem("o_rw_stored"), 16)

        def evac_wait(e, c, it=None, per=0):
            e.wait_ge(s_used, at(c + 1, it, per))

        def act_B(e):
            split_H(e, 0)
            split_H(e, 1)
            e.wait_ge(s_masks, 1)
            for c, dst in ((0, None), (1, None)):
                evac_wait(e, c)
                if c:
                    e.wait_ge(s_lxv, 2)
                e.activation(xs[:, 1:S + 1], bank2(2 * c), ACT.Copy).then_inc(s_evac, 1)
                e.wait_ge(s_lxv, 2 * c + 2)
                split_H(e, 2 + c)
                if c == 0:
                    e.activation(lx[0:64, :], lx[0:64, :], ACT.Tanh).then_inc(sem("lx_ready"), 1)
                else:
                    e.activation(sg[:, :], sg[:, :], ACT.Sigmoid).then_inc(sem("lx_ready"), 1)
            with e.Fori(0, NPAIR) as p:
                U = lambda i: (2 + i, p, UPB)
                n_mix = sem("mixed")
                for i in range(3):
                    if i:
                        split_H(e, *U(i + 1))
                    evac_wait(e, *U(i))
                    if i:
                        e.wait_ge(n_mix, at(i, p, 3))
                    else:
                        e.wait_ge(s_pv, p + 1)
                        wu, au, gu = a["w_up"][0], a["a_up"][0], a["g_up"][0]
                        e.dma_start(lora[0:64, 0, :], wu[:, bass.ds(p * P, P)]).then_inc(s_lora, 16)
                        e.dma_start(lora[64:P, 0, :], au[:, bass.ds(p * P, P)]).then_inc(s_lora, 16)
                        e.dma_start(lora[:, 1, :], gu[:, bass.ds(p * P, P)]).then_inc(s_lora, 16)
                    e.activation(xs[:, 1:S + 1], bank2(tile_bank[i]), ACT.Copy).then_inc(s_evac, 1)
                e.wait_ge(sem("lora_w_product"), p + 1)
                e.activation(lsum[:, :], bank2(4), ACT.Sigmoid, bias=pv[:, 3:4]).then_inc(sem("w_sigmoid"), 1)
                e.wait_ge(sem("lora_a_product"), p + 1)
                e.activation(a_[:, :], bank2(0), ACT.Sigmoid, bias=pv[:, 4:5]).then_inc(sem("a_sigmoid"), 1)
                split_H(e, *U(4))
                evac_wait(e, *U(3))
                e.activation(qf[:, :], bank2(tile_bank[3]), ACT.Copy, scale=HD ** -0.5).then_inc(s_evac, 1)
                e.wait_ge(sem("kk_scaled"), p + 1)
                e.activation(sq[:, :], kk[:, :], ACT.Square).then_inc(sem("norm_squares"), 1)
                split_H(e, *U(5))
                evac_wait(e, *U(4))
                e.activation(kf[:, :], bank2(tile_bank[4]), ACT.Copy).then_inc(s_evac, 1)
                e.wait_ge(sem("norm_sums"), p + 1)
                e.activation(sq[:, :], bank2(4), ACT.Sqrt).then_inc(sem("norm_root"), 1)
                e.preload_act_table_set("natural_log_exp_and_others")
                e.wait_ge(sem("decay_scanned"), p + 1)
                lc = lsum[:, :].rearrange("p (c t) -> p c t", t=CH)
                e.activation(elx[:, :, 1:CH + 1], lc, ACT.Exp, scale=-DECAY).then_inc(sem("decay_exps"), 1)
                e.activation(enl[:, :], lsum[:, :], ACT.Exp, scale=DECAY).then_inc(sem("decay_exps"), 1)
                split_H(e, *U(6))
                evac_wait(e, *U(5))
                e.activation(vf[:, :], bank2(tile_bank[5]), ACT.Copy).then_inc(s_evac, 1)
                e.wait_ge(sem("v_att_turned"), p + 1)
                e.activation(vt[:, :], bank2(2), ACT.Copy).then_inc(sem("v_att_tok"), 1)

                steps = Chain(e, sem("att_steps"), p, 2 * NA)

                def soft(s):
                    h, qh, kb = ATT[s]
                    lo = q_lo(qh, kb)
                    t = na[s % 2][:, lo:HALF]
                    e.wait_ge(sem("qk_product"), at(s + 1, p, NA))
                    if s >= 2:
                        e.wait_ge(sem("softplus_written"), at(s - 1, p, NA))
                    steps(e.activation(t, PS[:, z_bank(s), lo:HALF], ACT.Abs))
                    steps(e.activation(t, t, ACT.Exp, scale=-1.0))
                    e.activation(t, t, ACT.Ln, bias=1.0).then_inc(sem("att_ln"), 1)

                def weights(s):
                    h, qh, kb = ATT[s]
                    lo = q_lo(qh, kb)
                    e.wait_ge(sem("exponent_summed"), at(s + 1, p, NA))
                    if s >= 2:
                        e.wait_ge(sem("weights_used"), at(s - 1, p, NA))
                    e.activation(wt[s % 2][:, lo:HALF], PS[:, z_bank(s), lo:HALF], ACT.Exp)\
                        .then_inc(sem("weights_written"), 1)

                def o_out(s):
                    h, qh, kb = ATT[s]
                    if kb == 0:
                        g = 2 * h + qh
                        e.wait_ge(sem("weights_used"), at(s + 1, p, NA))
                        e.activation(ot[h * HD:(h + 1) * HD, qh * HALF:(qh + 1) * HALF],
                                     PS[h * HD:(h + 1) * HD, o_bank(g), :], ACT.Copy)\
                            .then_inc(sem("o_att_taken"), 1)

                soft(0)
                for s in range(NA):
                    if s + 1 < NA:
                        soft(s + 1)
                    weights(s)
                    if s:
                        o_out(s - 1)
                o_out(NA - 1)

                for i, dst in enumerate((tokA, tokB, tokK, tokV)):
                    if i == 0:
                        e.wait_ge(sem("o_att_stored"), at(16, p, 16))
                    e.wait_ge(sem("rw_turned"), at(i + 1, p, 4))
                    e.activation(dst[:, :, :].rearrange("p b f -> p (b f)"), bank2(2 * i), ACT.Copy)\
                        .then_inc(sem("rw_tok"), 1)
                n_t, n_tt = 0, 0
                for bq in range(2):
                    for l in range(6):
                        for h in range(2):
                            x = 3 * h
                            if 1 <= l <= 4:
                                n_t += 1
                                e.wait_ge(sem("inv_product"), at(n_t, p, 16))
                                e.activation(tm[h][:, :, :], PS[:, x + 1, :].rearrange("p (b t) -> p b t", t=P),
                                             ACT.Copy).then_inc(sem("inv_taken"), 1)
                            n_tt += 1
                            e.wait_ge(sem("inv_t_product"), at(n_tt, p, 24))
                            e.activation(tmT[h][:, :, :], PS[:, x + 2, :].rearrange("p (b t) -> p b t", t=P),
                                         ACT.Copy).then_inc(sem("inv_t_taken"), 1)
                split_H(e, *U(7))
                e.wait_ge(sem("y_block_summed"), at(NB, p, NB))
                e.activation(yt, bank2(6), ACT.Copy).then_inc(sem("y_taken"), 1)
                e.wait_ge(sem("g_product"), p + 1)
                e.activation(gg[:, :], bank2(2), ACT.Copy).then_inc(sem("g_taken"), 1)
                e.wait_ge(sem("y_centred"), p + 1)
                e.activation(yt, dt[:, :], ACT.Square).then_inc(sem("y_squared"), 1)
                e.wait_ge(sem("y_var_sums"), p + 1)
                e.activation(yt, bank2(0), ACT.Sqrt, scale=1.0 / HD, bias=eps[:, 1:2]).then_inc(sem("y_std"), 1)

        def dve_B(e):
            split_L(e, 0)
            split_L(e, 1)
            for c, dst in ((0, lx), (1, sg)):
                e.wait_ge(s_evac, c + 1)
                e.tensor_tensor(dt[:, :], xs[:, 0:S], xs[:, 1:S + 1], ALU.subtract).then_inc(s_lxv, 1)
                e.wait_ge(s_lxv, 2 * c + 1)
                e.scalar_tensor_tensor(out=dst[:, :], in0=dt[:, :], scalar=cols[:, C_MU2 + c:C_MU2 + c + 1],
                                       in1=xs[:, 1:S + 1], op0=ALU.mult, op1=ALU.add).then_inc(s_lxv, 1)
                e.wait_ge(s_lxv, 2 * c + 2)
                split_L(e, 2 + c)
            K = 17
            with e.Fori(0, NPAIR) as p:
                U = lambda i: (2 + i, p, UPB)
                ch = Chain(e, sem("dve_steps_B"), p, K)
                e.tensor_copy(pv[:, :], cols[:, bass.ds(p * PV + C_PAIR, PV)]).then_inc(s_pv, 1)
                e.wait_ge(s_pv, p + 1)
                for i, dst in enumerate((r_, k_, v_)):
                    if i:
                        split_L(e, *U(i + 1))
                    e.wait_ge(s_evac, at(2 + i + 1, p, UPB))
                    ch(e.tensor_tensor(dt[:, :], xs[:, 0:S], xs[:, 1:S + 1], ALU.subtract))
                    e.scalar_tensor_tensor(out=dst[:, :], in0=dt[:, :], scalar=pv[:, i:i + 1],
                                           in1=xs[:, 1:S + 1], op0=ALU.mult, op1=ALU.add).then_inc(sem("mixed"), 1)
                    e.wait_ge(sem("mixed"), at(i + 1, p, 3))
                e.tensor_scalar(kk[:, :], k_[:, :], pv[:, 5:6], None, ALU.mult).then_inc(sem("kk_scaled"), 1)
                split_L(e, *U(4))
                e.wait_ge(sem("w_sigmoid"), p + 1)
                e.tensor_tensor_scan(lsum[:, :], chunk_keep[:, :], lsum[:, :], 0.0, ALU.mult, ALU.add)\
                    .then_inc(sem("decay_scanned"), 1)
                e.wait_ge(sem("a_sigmoid"), p + 1)
                ch(e.tensor_scalar(dt[:, :], a_[:, :], -1.0, pv[:, 6:7], ALU.add, ALU.mult))
                ch(e.scalar_tensor_tensor(out=k_[:, :], in0=dt[:, :], scalar=1.0, in1=k_[:, :],
                                          op0=ALU.add, op1=ALU.mult))
                e.scalar_tensor_tensor(out=dt[:, :], in0=r_[:, :], scalar=pv[:, 7:8], in1=k_[:, :],
                                       op0=ALU.mult, op1=ALU.mult).then_inc(sem("rk_written"), 1)
                split_L(e, *U(5))
                e.wait_ge(sem("norm_root"), p + 1)
                ch(e.tensor_scalar(sq[:, :], sq[:, :], KK_FLOOR, None, ALU.max))
                ch(e.reciprocal(sq[:, :], sq[:, :]))
                e.wait_ge(sem("norm_squares"), p + 1)
                ch(e.tensor_tensor(kk[:, :], kk[:, :], sq[:, :], ALU.mult))
                e.wait_ge(sem("decay_exps"), 2 * p + 2)
                c3 = lambda t: t[:, :].rearrange("p (c t) -> p c t", t=CH)
                ch(e.scalar_tensor_tensor(out=c3(at_), in0=c3(kk), scalar=-1.0, in1=elx[:, :, 0:CH],
                                          op0=ALU.mult, op1=ALU.mult))
                ch(e.tensor_tensor(bt[:, :], kk[:, :], a_[:, :], ALU.mult))
                split_L(e, *U(6))
                ch(e.tensor_tensor(bt[:, :], bt[:, :], enl[:, :], ALU.mult))
                ch(e.tensor_tensor(kt_[:, :], k_[:, :], enl[:, :], ALU.mult))
                ch(e.tensor_tensor(c3(rt), c3(r_), elx[:, :, 1:CH + 1], ALU.mult))
                e.wait_ge(sem("bonus_sums"), p + 1)
                e.tensor_tensor(bv[:, :], bank2(0), v_[:, :], ALU.mult).then_inc(sem("rw_prepared"), 1)
                e.wait_ge(sem("rw_prepared"), p + 1)

                def softplus(s):
                    h, qh, kb = ATT[s]
                    lo = q_lo(qh, kb)
                    e.wait_ge(sem("att_ln"), at(s + 1, p, NA))
                    if s >= 2:
                        e.wait_ge(sem("exponent_summed"), at(s - 1, p, NA))
                        if sum_no[s - 2] > 0:
                            e.wait_ge(sem("softplus_summed"), at(sum_no[s - 2], p, NS_))
                    e.scalar_tensor_tensor(out=sp_[s % 2][:, lo:HALF], in0=PS[:, z_bank(s), lo:HALF], scalar=0.0,
                                           in1=na[s % 2][:, lo:HALF], op0=ALU.max, op1=ALU.add)\
                        .then_inc(sem("softplus_written"), 1)

                for s in range(NA):
                    softplus(s)

                n_q = 0
                m4 = lambda m: m.rearrange("p (o t) -> p o t", o=1).to_broadcast([P, 4, P])
                b4 = lambda b: PS[:, b, :].rearrange("p (b t) -> p b t", t=P)
                for bq in range(2):
                    for h in range(2):
                        n = 2 * bq + h
                        e.wait_ge(sem("n_ab_product"), at(n + 1, p, 4))
                        e.tensor_tensor(nab[h][:, :, :], b4(3 * h), m4(mask_upper[:, :]), ALU.mult)\
                            .then_inc(sem("n_ab_taken"), 1)
                        e.wait_ge(sem("n_ak_product"), at(n + 1, p, 4))
                        e.tensor_tensor(nak[h][:, :, :], b4(3 * h + 1), m4(mask_upper[:, :]), ALU.mult)\
                            .then_inc(sem("n_ak_taken"), 1)
                    for l in range(6):
                        for h in range(2):
                            n_q += 1
                            e.wait_ge(sem("level_product"), at(n_q, p, 24))
                            dst = tm[h] if l == 0 else qm[h]
                            e.tensor_tensor(dst[:, :, :], b4(3 * h), m4(mask_lvl[:, l, :]), ALU.mult)\
                                .then_inc(sem("level_taken"), 1)
                    for h in range(2):
                        n = 2 * bq + h
                        e.wait_ge(sem("m_ak_v_product"), at(n + 1, p, 4))
                        e.tensor_copy(mv[h][:, :, :], PS[:, 3 * h + 1, 0:4 * HD].rearrange("p (b v) -> p b v", v=HD))\
                            .then_inc(sem("m_ak_v_taken"), 1)
                    for h in range(2):
                        n = 2 * bq + h
                        hs = slice(h * HD, (h + 1) * HD)
                        e.wait_ge(sem("z_u_product"), at(n + 1, p, 4))
                        zv = zt[:, :].rearrange("p (b f) -> p b f", f=P)
                        e.tensor_copy(zv[:, 4 * bq:4 * bq + 4, hs],
                                      PS[:, 3 * h, 0:4 * HD].rearrange("p (b v) -> p b v", v=HD))
                        e.tensor_copy(ut[hs, 4 * bq * P:(4 * bq + 4) * P], PS[hs, 3 * h + 2, :])\
                            .then_inc(sem("z_u_taken"), 1)
                e.memset(ss_[0][:, :], 0.0).then_inc(sem("state_written"), 1)
                zv = zt[:, :].rearrange("p (b f) -> p b f", f=P)
                sv = sa[:, :].rearrange("p (b f) -> p b f", f=P)

                def readout(b):
                    e.wait_ge(sem("n_r_product"), at(b + 1, p, NB))
                    if b >= 2:
                        e.wait_ge(sem("y_block_summed"), at(b - 1, p, NB))
                    for h in range(2):
                        ins = e.tensor_tensor(
                            nr[b % 2][h][:, :, :], PS[:, 2 + h, 0:2 * P].rearrange("p (b t) -> p b t", t=P),
                            mask_incl[:, :].rearrange("p (o t) -> p o t", o=1).to_broadcast([P, 2, P]), ALU.mult)
                    ins.then_inc(sem("n_r_taken"), 1)

                readout(0)
                for c in range(NCH):
                    b, cp = c // 2, c % 2
                    rs = slice(cp * CH, (cp + 1) * CH)
                    e.wait_ge(sem("sa_product"), at(c + 1, p, NCH))
                    e.tensor_tensor(sv[rs, b, :], PS[rs, 0, 0:P], zv[rs, b, :], ALU.add).then_inc(sem("sa_written"), 1)
                    if cp == 0 and b + 1 < NB:
                        readout(b + 1)
                    if c + 1 < NCH:
                        e.wait_ge(sem("state_product"), at(c + 1, p, NCH - 1))
                        e.scalar_tensor_tensor(out=ss_[(c + 1) % 2][:, :], in0=PS[:, 1, 0:P],
                                               scalar=elx[:, c, CH:CH + 1], in1=same_head[:, :],
                                               op0=ALU.mult, op1=ALU.mult).then_inc(sem("state_written"), 1)
                split_L(e, *U(7))
                e.wait_ge(sem("y_mean_sums"), p + 1)
                e.scalar_tensor_tensor(out=dt[:, :], in0=bank2(0), scalar=-1.0 / HD, in1=yt,
                                       op0=ALU.mult, op1=ALU.add).then_inc(sem("y_centred"), 1)
                e.wait_ge(sem("y_std"), p + 1)
                ch(e.reciprocal(yt, yt))
                ch(e.tensor_tensor(dt[:, :], dt[:, :], yt, ALU.mult))
                ch(e.tensor_scalar(dt[:, :], dt[:, :], pv[:, 8:9], pv[:, 9:10], ALU.mult, ALU.add))
                ch(e.tensor_tensor(dt[:, :], dt[:, :], bv[:, :], ALU.add))
                e.wait_ge(sem("g_taken"), p + 1)
                e.tensor_tensor(dt[:, :], dt[:, :], gg[:, :], ALU.mult).then_inc(sem("o_rw_written"), 1)
                e.wait_ge(sem("o_rw_stored"), at(16, p, 16))
                ch.end()

        def pe_B(e):
            e.wait_ge(sem("block_L"), since("A", "block_L", NB))
            dense(e, 0, 0)
            dense(e, 1, 2)
            dense(e, 2, tile_bank[0])
            e.wait_ge(sem("lx_ready"), 2)
            with e.Fori(0, NPAIR) as p:
                def unit(i):
                    if i > 1:
                        e.wait_ge(s_evac, at(2 + i - 1, p, UPB))
                    dense(e, 2 + i, tile_bank[i], p, UPB)

                def wide(bank, lhsT, rhs, start=True, stop=True, rows=slice(0, P)):
                    for half in range(2):
                        mm = e.matmul(PS[:, bank + half, :], lhsT, rhs[rows, half * HALF:(half + 1) * HALF],
                                      start=start, stop=stop)
                    return mm

                unit(1); unit(2)
                e.wait_ge(s_lora, 48 * p + 48)
                wide(4, lora[0:64, 0, :], lx, rows=slice(0, 64)).then_inc(sem("lora_w_product"), 1)
                wide(0, lora[64:P, 0, :], lx, rows=slice(64, P)).then_inc(sem("lora_a_product"), 1)
                unit(3)
                e.wait_ge(sem("norm_squares"), p + 1)
                wide(4, same_head[:, :], sq).then_inc(sem("norm_sums"), 1)
                unit(4)
                e.wait_ge(sem("rk_written"), p + 1)
                wide(0, same_head[:, :], dt).then_inc(sem("bonus_sums"), 1)
                unit(5)
                e.wait_ge(s_evac, at(2 + 6, p, UPB))
                for b in range(NB):
                    mm = e.transpose(PS[:, 2 + b // 4, (b % 4) * P:(b % 4 + 1) * P], vf[:, b * P:(b + 1) * P], ident[:, :])
                mm.then_inc(sem("v_att_turned"), 1)

                def z_of(s):
                    h, qh, kb = ATT[s]
                    lo = q_lo(qh, kb)
                    hs = slice(h * HD, (h + 1) * HD)
                    if s >= 3:
                        e.wait_ge(sem("weights_written"), at(s - 2, p, NA))
                    e.matmul(PS[:, z_bank(s), lo:HALF], kf[hs, kb * P:(kb + 1) * P],
                             qf[hs, qh * HALF + lo:(qh + 1) * HALF], start=True, stop=True)\
                        .then_inc(sem("qk_product"), 1)

                def exponent(s):
                    h, qh, kb = ATT[s]
                    lo = q_lo(qh, kb)
                    first = kb == 4 * qh + 3
                    if kb >= 4 * qh:
                        e.wait_ge(sem("softplus_masked"), at(diag_no[s], p, ND))
                    e.wait_ge(sem("softplus_written"), at(s + 1, p, NA))
                    if kb >= 4 * qh:
                        e.matmul(PS[:, z_bank(s), lo:lo + P], ident_b[:, :], bar_att[:, :],
                                 start=False, stop=False, skip_group_check=True)
                    mm = e.matmul(PS[:, z_bank(s), lo:HALF], neg_tri[:, :], sp_[s % 2][:, lo:HALF],
                                  start=False, stop=True, skip_group_check=True)
                    if not first:
                        plo = q_lo(qh, kb + 1)
                        e.wait_ge(sem("softplus_summed"), at(sum_no[s - 1], p, NS_))
                        mm = e.matmul(PS[:, z_bank(s), plo:HALF], neg_one[:, :], ssum[(s + 1) % 2][:, plo:HALF],
                                      start=False, stop=True, skip_group_check=True)
                    mm.then_inc(sem("exponent_summed"), 1)

                def use_weights(s):
                    h, qh, kb = ATT[s]
                    lo = q_lo(qh, kb)
                    g = 2 * h + qh
                    first = kb == 4 * qh + 3
                    if first and g >= 2:
                        e.wait_ge(sem("o_att_taken"), at(g - 1, p, 4))
                    e.wait_ge(sem("weights_written"), at(s + 1, p, NA))
                    e.matmul(PS[h * HD:(h + 1) * HD, o_bank(g), lo:HALF],
                             vt[:, kb * P + h * HD:kb * P + (h + 1) * HD], wt[s % 2][:, lo:HALF],
                             start=first, stop=(kb == 0), skip_group_check=True).then_inc(sem("weights_used"), 1)

                z_of(0)
                z_of(1)
                e.wait_ge(sem("v_att_tok"), p + 1)
                for s in range(NA):
                    exponent(s)
                    if s:
                        use_weights(s - 1)
                    if s + 2 < NA:
                        z_of(s + 2)
                use_weights(NA - 1)

                e.wait_ge(sem("rw_prepared"), p + 1)
                e.wait_ge(sem("weights_written"), at(NA, p, NA))
                e.wait_ge(sem("o_att_taken"), at(4, p, 4))
                for i, src in enumerate((at_, bt, kt_, v_)):
                    for b in range(NB):
                        mm = e.transpose(PS[:, 2 * i + b // 4, (b % 4) * P:(b % 4 + 1) * P],
                                         src[:, b * P:(b + 1) * P], ident[:, :])
                    mm.then_inc(sem("rw_turned"), 1)
                e.wait_ge(sem("rw_tok"), at(4, p, 4))
                blk = lambda b: slice(b * P, (b + 1) * P)
                n_q = 0
                for bq in range(2):
                    for h in range(2):
                        n, x, hs = 2 * bq + h, 3 * h, slice(h * HD, (h + 1) * HD)
                        if bq:
                            e.wait_ge(sem("z_u_taken"), at(h + 1, p, 4))
                        for j in range(4):
                            mm = e.matmul(PS[:, x, blk(j)], bt[hs, blk(4 * bq + j)], at_[hs, blk(4 * bq + j)],
                                          start=True, stop=True)
                        mm.then_inc(sem("n_ab_product"), 1)
                        for j in range(4):
                            mm = e.matmul(PS[:, x + 1, blk(j)], kt_[hs, blk(4 * bq + j)], at_[hs, blk(4 * bq + j)],
                                          start=True, stop=True)
                        mm.then_inc(sem("n_ak_product"), 1)
                    for l in range(6):
                        for h in range(2):
                            n, x = 2 * bq + h, 3 * h
                            if l == 0:
                                e.wait_ge(sem("n_ab_taken"), at(n + 1, p, 4))
                            elif l == 1:
                                e.wait_ge(sem("level_taken"), at(12 * bq + h + 1, p, 24))
                            else:
                                e.wait_ge(sem("inv_taken"), at(8 * bq + 2 * (l - 2) + h + 1, p, 16))
                            e.matmul(PS[:, x, :], ident_b[:, :],
                                     ident_b[:, :].rearrange("p (o t) -> p o t", o=1).to_broadcast([P, 4, P]),
                                     start=True, stop=False, skip_group_check=True)
                            for j in range(4):
                                mm = e.matmul(PS[:, x, blk(j)], nab[h][:, j, :],
                                              ident[:, :] if l == 0 else tm[h][:, j, :],
                                              start=False, stop=True, skip_group_check=True)
                            mm.then_inc(sem("level_product"), 1)
                        for h in range(2):
                            n, x = 2 * bq + h, 3 * h
                            e.wait_ge(sem("level_taken"), at(12 * bq + 2 * l + h + 1, p, 24))
                            if l == 0:
                                for j in range(4):
                                    mm = e.transpose(PS[:, x + 2, blk(j)], tm[h][:, j, :], ident[:, :])
                                mm.then_inc(sem("inv_t_product"), 1)
                                continue
                            e.wait_ge(sem("inv_t_taken"), at(12 * bq + 2 * (l - 1) + h + 1, p, 24))
                            if l < 5:
                                if l == 1:
                                    e.wait_ge(sem("n_ak_taken"), at(n + 1, p, 4))
                                for j in range(4):
                                    mm = e.matmul(PS[:, x + 1, blk(j)], tmT[h][:, j, :], qm[h][:, j, :],
                                                  start=True, stop=True)
                                mm.then_inc(sem("inv_product"), 1)
                            for j in range(4):
                                mm = e.matmul(PS[:, x + 2, blk(j)], qm[h][:, j, :], tmT[h][:, j, :],
                                              start=True, stop=True)
                            mm.then_inc(sem("inv_t_product"), 1)
                    vv = lambda j, hs: tokV[:, 4 * bq + j, hs]
                    for h in range(2):
                        n, x, hs = 2 * bq + h, 3 * h, slice(h * HD, (h + 1) * HD)
                        e.wait_ge(sem("inv_taken"), at(8 * bq + 6 + h + 1, p, 16))
                        for j in range(4):
                            mm = e.matmul(PS[:, x + 1, j * HD:(j + 1) * HD], nak[h][:, j, :], vv(j, hs),
                                          start=True, stop=True)
                        mm.then_inc(sem("m_ak_v_product"), 1)
                    for h in range(2):
                        n, x, hs = 2 * bq + h, 3 * h, slice(h * HD, (h + 1) * HD)
                        e.wait_ge(sem("inv_t_taken"), at(12 * bq + 10 + h + 1, p, 24))
                        e.wait_ge(sem("m_ak_v_taken"), at(n + 1, p, 4))
                        for j in range(4):
                            e.matmul(PS[:, x, j * HD:(j + 1) * HD], tmT[h][:, j, :], mv[h][:, j, :],
                                     start=True, stop=True)
                        for j in range(4):
                            mm = e.matmul(PS[hs, x + 2, blk(j)], tokA[:, 4 * bq + j, hs], tmT[h][:, j, :],
                                          start=True, stop=True)
                        mm.then_inc(sem("z_u_product"), 1)

                sv = sa[:, :].rearrange("p (b f) -> p b f", f=P)

                def readout(b):
                    if b:
                        e.wait_ge(sem("n_r_taken"), at(b, p, NB))
                    for h in range(2):
                        hs = slice(h * HD, (h + 1) * HD)
                        e.matmul(PS[:, 2 + h, 0:P], bt[hs, blk(b)], rt[hs, blk(b)], start=True, stop=True)
                        mm = e.matmul(PS[:, 2 + h, P:2 * P], kt_[hs, blk(b)], rt[hs, blk(b)], start=True, stop=True)
                    mm.then_inc(sem("n_r_product"), 1)

                e.wait_ge(sem("z_u_taken"), at(4, p, 4))
                readout(0)
                for c in range(NCH):
                    b, cp = c // 2, c % 2
                    rs = slice(cp * CH, (cp + 1) * CH)
                    st = ss_[c % 2]
                    e.wait_ge(sem("state_written"), at(c + 1, p, NCH))
                    e.matmul(PS[rs, 0, 0:P], ut[:, c * CH:(c + 1) * CH], st[:, :], start=True, stop=True)\
                        .then_inc(sem("sa_product"), 1)
                    if c + 1 < NCH:
                        e.matmul(PS[:, 1, 0:P], ident[:, :], st[:, :], start=True, stop=False, skip_group_check=True)
                        e.matmul(PS[:, 1, 0:P], tokK[rs, b, :], tokV[rs, b, :], start=False, stop=False,
                                 skip_group_check=True)
                    e.matmul(PS[:, 6 + b // 4, (b % 4) * P + cp * CH:(b % 4) * P + (cp + 1) * CH], st[:, :],
                             rt[:, c * CH:(c + 1) * CH], start=(c % 8 == 0), stop=False, skip_group_check=True)
                    e.wait_ge(sem("sa_written"), at(c + 1, p, NCH))
                    if c + 1 < NCH:
                        e.matmul(PS[:, 1, 0:P], tokB[rs, b, :], sv[rs, b, :], start=False, stop=True,
                                 skip_group_check=True).then_inc(sem("state_product"), 1)
                    dense_piece(e, 2 + UPB, tile_bank[0], c // 2, c % 2, p, UPB)
                    if cp == 0 and b + 1 < NB:
                        readout(b + 1)
                    if cp == 1:
                        e.wait_ge(sem("n_r_taken"), at(b + 1, p, NB))
                        for h in range(2):
                            hs = slice(h * HD, (h + 1) * HD)
                            yo = PS[hs, 6 + b // 4, (b % 4) * P:(b % 4 + 1) * P]
                            e.matmul(yo, sv[:, b, hs], nr[b % 2][h][:, 0, :], start=False, stop=False,
                                     skip_group_check=True)
                            mm = e.matmul(yo, tokV[:, b, hs], nr[b % 2][h][:, 1, :], start=False, stop=True,
                                          skip_group_check=True)
                        mm.then_inc(sem("y_block_summed"), 1)
                wide(2, lora[:, 1, :], sg).then_inc(sem("g_product"), 1)
                e.wait_ge(sem("y_taken"), p + 1)
                wide(0, same_head[:, :], yt).then_inc(sem("y_mean_sums"), 1)
                e.wait_ge(sem("y_squared"), p + 1)
                wide(0, same_head[:, :], yt).then_inc(sem("y_var_sums"), 1)

        UC = 3 + NPAIR * UPB
        s_o = [sem(f"x_blocks{i}_loaded") for i in range(4)]
        s_w2 = sem("second_half_loaded")
        s_merged = sem("merged_written")

        def sp_C(e):
            with e.Fori(0, NPAIR) as j:
                for i in range(6):
                    c, m = UC + i, j * (2 * P) + (i // 3) * P
                    if i % 3 < 2:
                        load_unit(e, c, w_in[:, :, bass.ds(m + GATE_COL0 + (i % 3) * D, P)], j, 6)
                    else:
                        load_unit(e, c, w_sb[:, :, bass.ds(m, P)], j, 6, dst=raw[c % 2][:, 0:4, :])
                        e.dma_start(raw[c % 2][:, 4:8, :], w_rw[:, :, bass.ds(m, P)]).then_inc(s_w2, 16)

        def act_C(e):
            e.wait_ge(sem("o_att_stored"), 16 * NPAIR)
            e.wait_ge(sem("o_rw_stored"), 16 * NPAIR)
            for i in range(4):
                e.dma_start(mg[:, 2 * i:2 * i + 2, :], o_scr[2 * i:2 * i + 2].rearrange("k p t -> p k t"))\
                    .then_inc(s_o[i], 16)
            for k in range(KT):
                e.wait_ge(s_o[k // 2], 32)
                e.activation(oH[:, k, :], mg[:, k, :], ACT.Copy).then_inc(sem("o_H_written"), 1)
            with e.Fori(0, NPAIR) as j:
                for i in range(6):
                    c, u = UC + i, i // 3
                    if (i + 1) % 3 == 2:
                        e.wait_ge(s_w2, at(16 * (u + 1), j, 32))
                    split_H(e, c + 1, j, 6)
                    if i % 3 < 2:
                        evac_wait(e, c, j, 6)
                        e.wait_ge(s_merged, at(u + 1, j, 2))
                        bg = pg[:, (i % 3) * 2 + u:(i % 3) * 2 + u + 1]
                        if i == 0:
                            e.wait_ge(sem("gate_bias_set"), j + 1)
                        e.activation((g_sb, g_rw)[i % 3][:, :], bank2(2 * (i % 3)), ACT.Sigmoid, bias=bg)\
                            .then_inc(sem("gate_written"), 1)

        def dve_C(e):
            for k in range(KT):
                e.wait_ge(sem("o_H_written"), k + 1)
                ins = e.tensor_tensor(oL[:, k, :], mg[:, k, :], f32(oH[:, k, :]), ALU.subtract)
                if k < KT - 1:
                    ins.then_inc(sem("o_L_written"), 1)
            ins.then_inc(s_merged, 1)
            with e.Fori(0, NPAIR) as j:
                e.wait_ge(s_merged, at(1, j, 2))
                v = cols[:, C_BGATE:C_BGATE + 2 * KT].rearrange("p (a m) -> p a m", a=2)
                e.tensor_copy(pg[:, :].rearrange("p (a u) -> p a u", a=2), v[:, :, bass.ds(j * 2, 2)])\
                    .then_inc(sem("gate_bias_set"), 1)
                for i in range(6):
                    c, u = UC + i, i // 3
                    split_L(e, c + 1, j, 6)
                    if i % 3 == 2:
                        e.wait_ge(sem("gate_written"), at(2 * u + 2, j, 4))
                        evac_wait(e, c, j, 6)
                        e.tensor_tensor(g_sb[:, :], g_sb[:, :], bank2(4), ALU.mult).then_inc(sem("branch_gated"), 1)
                        e.tensor_tensor(g_rw[:, :], g_rw[:, :], bank2(6), ALU.mult).then_inc(sem("branch_gated"), 1)
                        e.wait_ge(sem("branch_gated"), at(2 * u + 2, j, 4))
                        e.tensor_tensor(mg[:, bass.ds(j * 2 + u, 1), :].rearrange("p o t -> p (o t)"),
                                        g_sb[:, :], g_rw[:, :], ALU.add).then_inc(s_merged, 1)

        def pe_C(e):
            e.wait_ge(s_merged, 1)
            with e.Fori(0, NPAIR) as j:
                for i in range(6):
                    c, u = UC + i, i // 3
                    if i % 3 < 2:
                        if i < 2:
                            e.wait_ge(s_merged, at(1, j, 2))
                        if i >= 3:
                            e.wait_ge(sem("gate_written"), at(i - 2, j, 4))
                        mm = dense(e, c, 2 * (i % 3), j, 6)
                    else:
                        e.wait_ge(s_merged, at(u + 1, j, 2))
                        dense(e, c, 4, j, 6, ks=range(0, 4), xH=oH, xL=oL, last=False)
                        dense(e, c, 6, j, 6, ks=range(4, 8), xH=oH, xL=oL)

        def rows_of(t):
            return t[:, :, :].rearrange("p k c -> p (k c)")

        def sp_rows(e, U0, w):
            for n in range(2 * KT):
                load_unit(e, U0 + n, w[:, n % KT, :], dst=rows_of(raw[(U0 + n) % 2]))

        def pe_rows(e, tag, U0, xH, xL):
            for n in range(2 * KT):
                c, t, k = U0 + n, n // KT, n % KT
                e.wait_ge(s_wL, c + 1)
                for b in range(4):
                    if t == 1 and k == 0:
                        e.wait_ge(sem("y_copied"), since(tag, "y_copied", b + 1))
                    mm = dense_rows(e, rows_of(wH[c % 2]), rows_of(wL[c % 2]), k, 2 * b, 4 * t + b,
                                    k == 0, k == KT - 1, xH, xL)
                    if k == KT - 1:
                        if b == 3:
                            mm.then_inc(s_used, 1)
                        else:
                            mm.then_inc(sem("y_done"), 1)
                    elif b == 3:
                        mm.then_inc(s_used, 1)

        def res_dma(e, tag, src, dst, bufs, gain=None):
            if gain is not None:
                e.dma_start(bufs[5][:, :], gain.partition_broadcast(P)).then_inc(sem("gain_loaded"), 16)
            for b in range(2):
                e.dma_start(bufs[1][b][:, :], src[:, b, :]).then_inc(sem(f"x_loaded{b}"), 16)
            for b in range(NB):
                e.wait_ge(sem("x_new"), since(tag, "x_new", b + 1))
                if dst is not None:
                    e.dma_start(dst[:, b, :], bufs[2][b % 2][:, :]).then_inc(sem(f"x_stored{b % 2}"), 16)
                if b + 2 < NB:
                    e.dma_start(bufs[1][b % 2][:, :], src[:, b + 2, :]).then_inc(sem(f"x_loaded{b % 2}"), 16)

        def y_of(bufs, b, yacc_):
            return (bufs[3] if yacc_ is None else yacc_)[:, b, :]

        def act_copy(e, tag, b, bufs, U0):
            if b % 4 == 3:
                e.wait_ge(s_used, U0 + (1 + b // 4) * KT)
            else:
                e.wait_ge(sem("y_done"), since(tag, "y_done", 3 * (b // 4) + b % 4 + 1))
            e.activation(bufs[3][:, b, :], bank2(2 * (b % 4)), ACT.Copy).then_inc(sem("y_copied"), 1)

        def pipelined(b, first, end, part1, part2):
            if b == first and part1:
                part1(b)
            if b + 1 < end and part1:
                part1(b + 1)
            part2(b)

        def block_summed(e, tag, b):
            e.wait_ge(sem("y_added"), since(tag, "y_added", 8 * NG + b + 1))

        def act_stats(e, tag, b, bufs, yacc_, first):
            if yacc_ is None:
                e.wait_ge(sem("y_copied"), since(tag, "y_copied", b + 1))
            else:
                block_summed(e, tag, b)
            done = b if b == first else b - 1
            if done:
                e.wait_ge(sem("squares2"), since(tag, "squares2", done))
            if b:
                e.wait_ge(sem("squares"), since(tag, "squares", b))
            e.activation(bufs[6], y_of(bufs, b, yacc_), ACT.Square, accum_out=ss[:, b:b + 1])\
                .then_inc(sem("squares"), 1)
            e.wait_ge(sem("squares"), since(tag, "squares", b + 1))
            e.activation(sd[:, b:b + 1], ss[:, b:b + 1], ACT.Sqrt, scale=1.0 / D, bias=eps[:, 0:1])\
                .then_inc(sem("std"), 1)

        def act_x(e, tag, b, bufs, stats_done=0):
            e.wait_ge(sem("x_new"), since(tag, "x_new", b + 1))
            if b:
                e.wait_ge(sem("squares2"), since(tag, "squares2", b))
            if stats_done:
                e.wait_ge(sem("squares"), since(tag, "squares", stats_done))
            e.activation(bufs[6], bufs[2][b % 2][:, :], ACT.Square, accum_out=ss2[:, b:b + 1])\
                .then_inc(sem("squares2"), 1)
            e.wait_ge(sem("squares2"), since(tag, "squares2", b + 1))
            e.activation(sd2[:, b:b + 1], ss2[:, b:b + 1], ACT.Sqrt, scale=1.0 / D, bias=eps[:, 0:1])\
                .then_inc(sem("std2"), 1)

        def dve_x(e, tag, b, bufs, yacc_, y_norm, stored=True):
            y, xr, x1 = y_of(bufs, b, yacc_), bufs[1][b % 2], bufs[2][b % 2]
            if yacc_ is not None:
                block_summed(e, tag, b)
            if y_norm:
                e.wait_ge(sem("std"), since(tag, "std", b + 1))
                if b == 0:
                    e.wait_ge(sem("gain_loaded"), since(tag, "gain_loaded", 16))
                e.reciprocal(rstd[:, b:b + 1], sd[:, b:b + 1]).then_inc(sem("rstd"), 1)
                e.wait_ge(sem("rstd"), since(tag, "rstd", b + 1))
                e.scalar_tensor_tensor(out=y, in0=y, scalar=rstd[:, b:b + 1], in1=bufs[5][:, :],
                                       op0=ALU.mult, op1=ALU.mult).then_inc(sem("y_gained"), 1)
                e.wait_ge(sem("y_gained"), since(tag, "y_gained", b + 1))
            elif yacc_ is None:
                e.wait_ge(sem("y_copied"), since(tag, "y_copied", b + 1))
            e.wait_ge(sem(f"x_loaded{b % 2}"), since(tag, f"x_loaded{b % 2}", 16 * (b // 2 + 1)))
            if b >= 2:
                if stored:
                    e.wait_ge(sem(f"x_stored{b % 2}"), since(tag, f"x_stored{b % 2}", 16 * (b // 2)))
                e.wait_ge(sem("block_normalised"), since(tag, "block_normalised", b - 1))
            e.tensor_tensor(x1[:, :], y, xr[:, :], ALU.add).then_inc(sem("x_new"), 1)

        def dve_h(e, tag, b, bufs):
            e.wait_ge(sem("std2"), since(tag, "std2", b + 1))
            e.reciprocal(rstd2[:, b:b + 1], sd2[:, b:b + 1]).then_inc(sem("rstd2"), 1)
            e.wait_ge(sem("rstd2"), since(tag, "rstd2", b + 1))
            e.tensor_scalar(bufs[3][:, b, :], bufs[2][b % 2][:, :], rstd2[:, b:b + 1], None, ALU.mult)\
                .then_inc(sem("block_normalised"), 1)

        def act_block(e, tag, b, first, end, bufs, yacc_, y_norm):
            pipelined(b, first, end, (lambda i: act_stats(e, tag, i, bufs, yacc_, first)) if y_norm else None,
                      lambda i: act_x(e, tag, i, bufs, min(i + 2, end) if y_norm else 0))

        def tail(bufs, block, turn):
            between = bufs is not for_G
            for b in range(4, NB):
                block(b)
                if between:
                    turn(b - 4)
            for b in range(4 if between else 0, NB):
                turn(b)

        def act_rows(e, tag, U0, bufs, y_norm):
            def block(b):
                act_block(e, tag, b, b // 4 * 4, b // 4 * 4 + 4, bufs, None, y_norm)

            for n in range(2 * KT):
                split_H(e, U0 + n + 1)
                if n == KT:
                    for b in range(4):
                        act_copy(e, tag, b, bufs, U0)
                if KT < n <= KT + 4:
                    block(n - KT - 1)
            for b in range(4, NB):
                act_copy(e, tag, b, bufs, U0)
            tail(bufs, block, lambda b: act_turn(e, tag, bufs, b))

        def dve_rows(e, tag, U0, bufs, y_norm, gcol):
            def block(b):
                pipelined(b, b // 4 * 4, b // 4 * 4 + 4, lambda i: dve_x(e, tag, i, bufs, None, y_norm),
                          lambda i: dve_h(e, tag, i, bufs))

            for n in range(2 * KT):
                split_L(e, U0 + n + 1)
                if KT < n <= KT + 4:
                    block(n - KT - 1)
            tail(bufs, block, lambda b: dve_turn(e, tag, bufs, gcol, b))

        def act_turn(e, tag, bufs, b):
            to_feature_H(e, tag, b, slice(b * P, (b + 1) * P), bufs[4])

        def dve_turn(e, tag, bufs, gcol, b):
            to_feature_gain(e, tag, b, gcol, bufs[4])
            to_feature_L(e, tag, b, slice(b * P, (b + 1) * P), bufs[4])

        def pe_turn(e, tag, bufs):
            e.wait_ge(sem("y_copied"), since(tag, "y_copied", NB))
            for b in range(NB):
                to_feature_pe(e, tag, bufs[3][:, b, :], b, b)

        UD = UC + 6 * NPAIR
        UE = UD + 2 * KT
        x_new_scr = {"D": x1_scr, "E": x2_scr}

        def act_D(e):
            e.wait_ge(s_merged, 2 * NPAIR + 1)
            evac_wait(e, UD - 1)
            for k in range(KT):
                e.activation(hH[:, k, :], mg[:, k, :], ACT.Copy).then_inc(sem("merged_H"), 1)
            e.wait_ge(sem("merged_L"), KT)
            act_rows(e, "D", UD, for_D, True)

        def dve_D(e):
            for k in range(KT):
                e.wait_ge(sem("merged_H"), k + 1)
                e.tensor_tensor(hL[:, k, :], mg[:, k, :], f32(hH[:, k, :]), ALU.subtract).then_inc(sem("merged_L"), 1)
            dve_rows(e, "D", UD, for_D, True, C_FPRE)

        def pe_D(e):
            e.wait_ge(sem("merged_L"), KT)
            pe_rows(e, "D", UD, hH, hL)
            pe_turn(e, "D", for_D)

        def sp_D(e):
            sp_rows(e, UD, w_o)

        def pool_D(e):
            e.wait_ge(sem("merged_L"), KT)
            res_dma(e, "D", x_tok, x1_scr, for_D, a["norm_mix_post"][0])

        UE_END = UE + 4 * NG

        def ffn_turns(e, turn):
            turn(None)
            with e.Fori(1, NG) as i:
                turn(i)

        def sp_ffn(e, tag, prev, U0, w_first, c_first, w_second, c_second, w_down):
            def turn(it):
                tile = lambda w, col, j: (w[:, :, col + j * P:col + (j + 1) * P] if it is None
                                          else w[:, :, bass.ds(it * (2 * P) + (col + j * P), P)])
                load_unit(e, U0, tile(w_first, c_first, 0), it, 4)
                load_unit(e, U0 + 1, tile(w_second, c_second, 0), it, 4)
                if it is None:
                    ffn_memory_free(e, prev)
                    e.dma_start(rawD[:, :, :], w_down[:, 0:2, :]).then_inc(sem("down_loaded"), 16)
                else:
                    e.wait_ge(sem("down_H"), since(tag, "down_H", it))
                    e.wait_ge(sem("down_L"), since(tag, "down_L", it))
                    e.sem_inc(s_held, 1)
                    e.dma_start(rawD[:, :, :], w_down[:, bass.ds(it * 2, 2), :])\
                        .then_inc(sem("down_loaded"), 16)
                load_unit(e, U0 + 2, tile(w_first, c_first, 1), it, 4)
                load_unit(e, U0 + 3, tile(w_second, c_second, 1), it, 4)

            ffn_turns(e, turn)

        def ffn_memory_free(e, prev):
            e.wait_ge(sem("block_L"), since(prev, "block_L", NB))
            for i in range(2):
                e.wait_ge(sem(f"x_stored{i}"), since(prev, f"x_stored{i}", 16 * (NB // 2)))

        def act_ffn(e, tag, prev, U0, conv):
            hid, silu = sem("hidden"), sem("silu")
            ffn_memory_free(e, prev)

            def turn(it):
                def conv_start(u, j):
                    if u:
                        e.wait_ge(silu, since(tag, "silu", at(j + 1, it, 2)))
                    elif j or it is not None:
                        e.wait_ge(hid, since(tag, "hidden", at(j, it, 2)))
                    o = 8 * j + (4 if u == 0 else 0)
                    e.wait_ge(sem(f"{tag}_conv_columns"), at(1, it, 1))
                    e.activation(cvo[:, :], bank2(2 * u), ACT.Identity, bias=cvt[:, o + 3:o + 4],
                                 scale=cvt[:, o + 2:o + 3]).then_inc(sem(f"{tag}_conv_started"), 1)

                for j in range(2):
                    c = U0 + 2 * j
                    split_H(e, c + 1, it, 4)
                    evac_wait(e, c, it, 4)
                    if conv:
                        conv_start(0, j)
                        e.wait_ge(sem(f"{tag}_conv_done"), at(2 * j + 1, it, 4))
                    elif j or it is not None:
                        e.wait_ge(hid, since(tag, "hidden", at(j, it, 2)))
                    e.activation(sil[:, :], cvo[:, :] if conv else bank2(0), ACT.Silu).then_inc(silu, 1)
                    split_H(e, c + 2, it, 4)
                    if conv:
                        evac_wait(e, c + 1, it, 4)
                        conv_start(1, j)
                    e.wait_ge(hid, since(tag, "hidden", at(j + 1, it, 2)))
                    if it is not None and j == 0:
                        e.wait_ge(sem("y_part"), since(tag, "y_part", at(0, it, 8)))
                    e.activation(hdH[:, j, :], hf[:, :], ACT.Copy).then_inc(sem("hidden_H"), 1)
                    if j == 0:
                        e.wait_ge(sem("down_loaded"), since(tag, "down_loaded", at(16, it, 16)))
                        e.activation(dH[:, :, :], rawD[:, :, :], ACT.Copy).then_inc(sem("down_H"), 1)

            ffn_turns(e, turn)

        def dve_ffn(e, tag, prev, U0, conv):
            hid, silu, added = sem("hidden"), sem("silu"), sem("y_added")
            ffn_memory_free(e, prev)
            for b in range(NB):
                e.memset(yacc[:, b, :], 0.0).then_inc(added, 1)

            def add(it, b, per=8, c=-7):
                e.wait_ge(sem("y_part"), since(tag, "y_part", at(b + c, it, per)))
                e.wait_ge(added, since(tag, "y_added", at(b + c, it, per)))
                e.tensor_tensor(yacc[:, b, :], yacc[:, b, :], bank2(4 + 2 * (b % 2)), ALU.add).then_inc(added, 1)

            def turn(it):
                def taps(u, j):
                    o, n = 8 * j + (4 if u == 0 else 0), 2 * j + u
                    x = bank2(2 * u)
                    e.wait_ge(sem(f"{tag}_conv_started"), at(n + 1, it, 4))
                    e.scalar_tensor_tensor(out=cvo[:, 1:S], in0=x[:, 0:S - 1], scalar=cvt[:, o + 1:o + 2],
                                           in1=cvo[:, 1:S], op0=ALU.mult, op1=ALU.add)\
                        .then_inc(sem(f"{tag}_conv_tap1"), 1)
                    e.wait_ge(sem(f"{tag}_conv_tap1"), at(n + 1, it, 4))
                    e.scalar_tensor_tensor(out=cvo[:, 2:S], in0=x[:, 0:S - 2], scalar=cvt[:, o:o + 1],
                                           in1=cvo[:, 2:S], op0=ALU.mult, op1=ALU.add)\
                        .then_inc(sem(f"{tag}_conv_done"), 1)

                if conv:
                    if it is not None:
                        e.wait_ge(hid, since(tag, "hidden", at(0, it, 2)))
                    e.tensor_copy(cvt[:, :], cols[:, C_CONV:C_CONV + 16] if it is None
                                  else cols[:, bass.ds(it * 16 + C_CONV, 16)])\
                        .then_inc(sem(f"{tag}_conv_columns"), 1)
                    e.wait_ge(sem(f"{tag}_conv_columns"), at(1, it, 1))
                for j in range(2):
                    c = U0 + 2 * j
                    split_L(e, c + 1, it, 4)
                    if conv:
                        taps(0, j)
                    if j == 0 and it is not None:
                        for b in range(NB):
                            add(it, b)
                    if j == 1:
                        e.wait_ge(sem("down_H"), since(tag, "down_H", at(1, it, 1)))
                        e.tensor_tensor(dL[:, :, :], rawD[:, :, :], f32(dH[:, :, :]), ALU.subtract)\
                            .then_inc(sem("down_L"), 1)
                    split_L(e, c + 2, it, 4)
                    if conv:
                        taps(1, j)
                        e.wait_ge(sem(f"{tag}_conv_done"), at(2 * j + 2, it, 4))
                    else:
                        evac_wait(e, c + 1, it, 4)
                    e.wait_ge(silu, since(tag, "silu", at(j + 1, it, 2)))
                    if j or it is not None:
                        e.wait_ge(sem("hidden_L"), since(tag, "hidden_L", at(j, it, 2)))
                    e.tensor_tensor(hf[:, :], cvo[:, :] if conv else bank2(2), sil[:, :], ALU.mult).then_inc(hid, 1)
                    e.wait_ge(sem("hidden_H"), since(tag, "hidden_H", at(j + 1, it, 2)))
                    e.tensor_tensor(hdL[:, j, :], hf[:, :], f32(hdH[:, j, :]), ALU.subtract)\
                        .then_inc(sem("hidden_L"), 1)

            ffn_turns(e, turn)
            return lambda b: add(None, b, c=8 * NG - 7)

        def pe_ffn(e, tag, prev, U0, conv):
            gate_taken = (lambda j, it: e.wait_ge(sem(f"{tag}_conv_done"), at(2 * j - 1, it, 4))) if conv else \
                (lambda j, it: e.wait_ge(sem("silu"), since(tag, "silu", at(j, it, 2))))
            up_taken = lambda j, it: e.wait_ge(sem("hidden"), since(tag, "hidden", at(j, it, 2)))

            def down(it, t=0):
                for b in range(NB):
                    down_block(it, t, b)

            def down_block(it, t, b):
                if b == 0:
                    e.wait_ge(sem("down_L"), since(tag, "down_L", at(t, it, 1)))
                    e.wait_ge(sem("hidden_L"), since(tag, "hidden_L", at(2 * t, it, 2)))
                e.wait_ge(sem("y_added"), since(tag, "y_added", at(8 * t + b - 1, it, 8)))
                for kt in range(2):
                    mm = dense_rows(e, dH[:, kt, :], dL[:, kt, :], kt, 4 + 2 * (b % 2), b,
                                    kt == 0, kt == 1, xH=hdH, xL=hdL)
                mm.then_inc(sem("y_part"), 1)

            def turn(it):
                if it is None:
                    e.wait_ge(sem("block_L"), since(prev, "block_L", NB))
                for j in range(2):
                    if j or it is not None:
                        gate_taken(j, it)
                    dense(e, U0 + 2 * j, 0, it, 4)
                    if j == 0 and it is not None:
                        down(it)
                    if j or it is not None:
                        up_taken(j, it)
                    dense(e, U0 + 2 * j + 1, 2, it, 4)

            ffn_turns(e, turn)
            return lambda b: down_block(None, NG, b)

        def staged(*parts):
            for i in range(NB + len(parts) - 1):
                for k, part in enumerate(parts):
                    if 0 <= i - k < NB:
                        part(i - k)

        def sp_E(e):
            sp_ffn(e, "E", "D", UE, w_g, 0, w_u, 0, w_d)

        def pool_E(e):
            ffn_memory_free(e, "D")
            res_dma(e, "E", x1_scr, x2_scr, for_E, a["norm_ffn_post"][0])

        def act_E(e):
            act_ffn(e, "E", "D", UE, False)
            staged(lambda b: act_stats(e, "E", b, for_E, yacc, 0),
                   lambda b: act_x(e, "E", b, for_E, min(b + 2, NB)),
                   lambda b: act_turn(e, "E", for_E, b))

        def dve_E(e):
            add = dve_ffn(e, "E", "D", UE, False)
            staged(add, lambda b: dve_x(e, "E", b, for_E, yacc, True),
                   lambda b: dve_h(e, "E", b, for_E),
                   lambda b: dve_turn(e, "E", for_E, C_GPRE2, b))

        def pe_E(e):
            down = pe_ffn(e, "E", "D", UE, False)
            staged(down, *[lambda b: None] * 2,
                   lambda b: to_feature_pe(e, "E", yacc[:, b, :], b, b))

        UF = UE_END
        UPF = 5
        ORDER_F = (4, 3, 0, 1, 2)
        NSF = 2 * NB
        STEPS_F = [(h, qb) for h in range(2) for qb in range(NB)]
        c_scr = nc.dram_tensor("c_scratch", [8 * S], F32, kind="Internal").ap()

        def pairs_F(e, pair):
            with e.Fori(0, NPAIR // 2) as j:
                for q in range(2):
                    pair(lambda x, per: at(x + q * per, j, 2 * per),
                         lambda base, size, count=1, step=1: bass.ds(j * (2 * step) + (base + q * step), size),
                         (UF + 1 + UPF * q, j, 2 * UPF))

        def unit_F(u, i):
            return (u[0] + i, u[1], u[2])

        def sp_F(e):
            c = UF % 2
            e.wait_ge(s_wH, UF - 1)
            e.wait_ge(s_wL, UF - 1)
            e.sem_inc(s_held, 1)
            e.dma_start(raw[c][:, :, 8:P], w_in2[:, :, 0:P - 8]).then_inc(sem("F_forget_rest"), 16)
            e.wait_ge(sem("F_forget_rest"), 16)
            e.dma_start(raw[c][:, :, 0:8], w_in2[:, :, 5 * HALF:5 * HALF + 8]).then_inc(s_raw[c], 16)

            def pair(n, ds, u):
                for i, part in enumerate(ORDER_F):
                    load_unit(e, *(unit_F(u, i)[:1]), w_in2[:, :, ds(part * HALF, P, step=P)], *(unit_F(u, i)[1:]))

            pairs_F(e, pair)

        def pool_F(e):
            ffn_memory_free(e, "E")
            ch = Chain(e, sem("mask_steps"), base=N_MASK_STEPS)
            ch(e.memset(same_F[:, :], 0.0))
            ch(e.memset(same_F[0:64, 0:64], 1.0))
            ch(e.memset(same_F[64:P, 64:P], 1.0))
            ch(e.memset(keep_F[:, :], 1.0))
            ch(e.affine_select(out=keep_F[:, :], in_=keep_F[:, :], compare_op=ALU.is_ge, fill=0.0, base=0,
                               pattern=[[1, P]], channel_multiplier=-1))
            ch(e.memset(bar_F[:, :], 0.0))
            ch(e.affine_select(out=bar_F[:, :], in_=bar_F[:, :], compare_op=ALU.is_ge, fill=-1e30, base=0,
                               pattern=[[-1, P]], channel_multiplier=1))
            e.tensor_copy(ident_F[:, :], ident[:, :]).then_inc(sem("masks_written"), 1)
            e.dma_start(b_fg[:, :], a["b_forget_2"][0].rearrange("(h o) -> h o", o=1))\
                .then_inc(sem("F_forget_bias_loaded"), 16)
            e.wait_ge(sem("F_c_summed"), 1)
            e.dma_start(c_scr.rearrange("(h t) -> h t", h=8), c_row[:, :]).then_inc(sem("F_c_stored"), 16)
            e.wait_ge(sem("F_c_stored"), 16)
            w_sp = a["w_spatial_2"][0].rearrange("g i j -> i g j")
            b_sp = a["b_spatial_2"][0].rearrange("g i -> (g i)")

            def pair(n, ds, u):
                e.wait_ge(sem("F_pair_done"), n(1, 1))
                e.dma_start(wsp[:, :, :], w_sp[:, ds(0, 2, step=2), :]).then_inc(sem("F_spatial_loaded"), 16)
                for h in range(2):
                    e.dma_start(bsp[h * HD:(h + 1) * HD, :], b_sp[ds(h * P, P, step=2 * P)].partition_broadcast(HD))\
                        .then_inc(sem("F_spatial_loaded"), 16)
                    e.dma_start(c_keys[h][:, :], c_scr[ds(h * S, S, step=2 * S)].partition_broadcast(P))\
                        .then_inc(sem("F_c_keys_loaded"), 16)

            pairs_F(e, pair)

        def act_F(e):
            ffn_memory_free(e, "E")
            split_H(e, UF + 1)
            evac_wait(e, UF)
            e.wait_ge(sem("F_forget_bias_loaded"), 16)
            ch = Chain(e, sem("att_steps"), base=2 * NA * NPAIR)
            ch(e.activation(f_abs, PS[0:8, 0:2, :].rearrange("p a n -> p (a n)"), ACT.Abs, bias=b_fg[:, 0:1]))
            ch(e.activation(f_abs, f_abs, ACT.Exp, scale=-1.0))
            e.activation(f_abs, f_abs, ACT.Ln, bias=1.0).then_inc(sem("F_forget_ln"), 1)
            e.wait_ge(sem("F_c_stored"), 16)
            e.wait_ge(sem("F_forget_taken"), 1)

            def pair(n, ds, u):
                def tile(i, dst):
                    split_H(e, *unit_F(u, i + 1))
                    evac_wait(e, *unit_F(u, i))
                    x = bank2(2 * (i % 2))
                    if i >= 2:
                        ins = e.activation(dst, x, ACT.Copy, scale=HD ** -0.5 if i == 2 else 1.0)
                    else:
                        ins = e.activation(dst, x, ACT.Gelu_apprx_tanh)
                    ins.then_inc(sem("dense_tile_taken"), 1)

                tile(0, vg_F)
                e.wait_ge(sem("dense_tile_taken"), since("F", "dense_tile_taken", n(1, 5)))
                e.activation(lg[0][:, :], vg_F, ACT.Square).then_inc(sem("norm_squares"), 1)
                tile(1, u_F)
                e.wait_ge(sem("norm_sums"), since("F", "norm_sums", n(1, 1)))
                e.activation(lg[0][:, :], bank2(4), ACT.Sqrt, scale=1.0 / HD, bias=eps[:, 0:1])\
                    .then_inc(sem("norm_root"), 1)
                tile(2, q_F)
                e.wait_ge(sem("F_vg_turned"), n(1, 1))
                e.activation(lg[1][:, :], bank2(4), ACT.Copy).then_inc(sem("F_vg_tok"), 1)
                tile(3, k_F)
                tile(4, v_F)
                e.wait_ge(sem("v_att_turned"), since("F", "v_att_turned", n(1, 1)))
                e.activation(vt_F[:, :], bank2(4), ACT.Copy).then_inc(sem("v_att_tok"), 1)
                e.wait_ge(sem("F_gated"), n(1, 1))
                e.activation(mixH[:, ds(NPAIR, 1), :].rearrange("p o t -> p (o t)"), lg[0][:, :], ACT.Copy)\
                    .then_inc(sem("F_gated_H"), 1)

                def exp(s):
                    h, qb = STEPS_F[s]
                    w = (qb + 1) * P
                    e.wait_ge(sem("F_row_max"), n(s + 1, NSF))
                    if s == 1:
                        e.wait_ge(sem("F_mixed"), n(1, 1))
                    e.activation(lg[s % 2][:, 0:w], lg[s % 2][:, 0:w], ACT.Exp, bias=nmax[:, s:s + 1],
                                 accum_out=den[:, den_col(s):den_col(s) + 1]).then_inc(sem("weights_written"), 1)

                def turned(s):
                    w = (STEPS_F[s][1] + 1) * P
                    e.wait_ge(sem("F_p_turned"), n(s + 1, NSF))
                    if s >= 2:
                        e.wait_ge(sem("weights_used"), since("F", "weights_used", n(s - 1, NSF)))
                    e.activation(pT[s % 2][:, 0:w], bank2(4)[:, 0:w], ACT.Copy).then_inc(sem("F_p_taken"), 1)

                exp(0)
                for s in range(NSF):
                    if s + 1 < NSF:
                        exp(s + 1)
                    turned(s)
                e.wait_ge(sem("F_den_turned"), n(1, 1))
                e.activation(lg[1][:, :], bank2(4), ACT.Copy).then_inc(sem("F_den_taken"), 1)
                e.wait_ge(sem("F_o_divided"), n(1, 1))
                e.activation(mixH[:, ds(0, 1), :].rearrange("p o t -> p (o t)"), lg[1][:, :], ACT.Copy)\
                    .then_inc(sem("F_att_H"), 1)

            pairs_F(e, pair)

        def dve_F(e):
            ffn_memory_free(e, "E")
            ch = Chain(e, sem("F_dve_steps"))
            ch(e.memset(c_keys[0][0:8, :], 1.0))
            split_L(e, UF + 1)
            evac_wait(e, UF)
            e.wait_ge(sem("F_forget_bias_loaded"), 16)
            e.wait_ge(sem("F_forget_ln"), 1)
            ch(e.tensor_scalar(f_log, PS[0:8, 0:2, :].rearrange("p a n -> p (a n)"), b_fg[:, 0:1], 0.0,
                               ALU.add, ALU.min))
            ch(e.tensor_tensor(f_log, f_log, f_abs, ALU.subtract))
            e.tensor_tensor_scan(c_row[:, :], c_keys[0][0:8, :], f_log, 0.0, ALU.mult, ALU.add)\
                .then_inc(sem("F_c_summed"), 1)
            e.wait_ge(sem("F_c_turned"), 1)
            e.tensor_copy(c_cols[:, :, :], PS[:, 4, 0:8 * NB].rearrange("p (b h) -> p b h", h=8))\
                .then_inc(sem("F_forget_taken"), 1)
            e.wait_ge(sem("F_forget_taken"), 1)
            e.sem_inc(sem("F_pair_done"), 1)

            K, before = 4 + NSF, ch.n

            def pair(n, ds, u):
                ch = Chain(e, sem("F_dve_steps"), value=lambda i: n(before + i, K))
                e.tensor_copy(c_q[:, :, :], c_cols[:, :, ds(0, 2, step=2)]).then_inc(sem("pair_vectors_set"), 1)
                e.tensor_copy(vg_gain[:, :], cols[:, ds(C_VG, 1)]).then_inc(sem("pair_vectors_set"), 1)
                split_L(e, *unit_F(u, 1))
                split_L(e, *unit_F(u, 2))
                e.wait_ge(sem("pair_vectors_set"), since("F", "pair_vectors_set", n(2, 2)))
                e.wait_ge(sem("norm_root"), since("F", "norm_root", n(1, 1)))
                ch(e.reciprocal(lg[0][:, :], lg[0][:, :]))
                e.scalar_tensor_tensor(out=vg_F, in0=vg_F, scalar=vg_gain[:, 0:1], in1=lg[0][:, :],
                                       op0=ALU.mult, op1=ALU.mult).then_inc(sem("F_vg_normalised"), 1)
                split_L(e, *unit_F(u, 3))
                e.wait_ge(sem("F_spatial_turned"), n(1, 1))
                e.tensor_tensor(wspT[:, :, :], PS[:, 6, 0:2 * P].rearrange("p (g i) -> p g i", g=2),
                                keep_F[:, :].rearrange("p (o i) -> p o i", o=1).to_broadcast([P, 2, P]), ALU.mult)\
                    .then_inc(sem("F_spatial_masked"), 1)
                split_L(e, *unit_F(u, 4))
                e.wait_ge(sem("F_mixed"), n(1, 1))
                e.wait_ge(sem("F_vg_normalised"), n(1, 1))
                e.wait_ge(sem("F_spatial_loaded"), n(48, 48))
                ch(e.tensor_tensor(lg[0][:, :].rearrange("p (b i) -> p b i", i=P),
                                   bank2(6).rearrange("p (b i) -> p b i", i=P),
                                   bsp[:, :].rearrange("p (o i) -> p o i", o=1).to_broadcast([P, NB, P]), ALU.add))
                e.tensor_tensor(lg[0][:, :], lg[0][:, :], u_F, ALU.mult).then_inc(sem("F_gated"), 1)
                split_L(e, *unit_F(u, 5))
                e.wait_ge(sem("F_gated_H"), n(1, 1))
                ch(e.tensor_tensor(mixL[:, ds(NPAIR, 1), :].rearrange("p o t -> p (o t)"), lg[0][:, :],
                                   f32(mixH[:, ds(NPAIR, 1), :].rearrange("p o t -> p (o t)")), ALU.subtract))
                e.wait_ge(sem("F_c_keys_loaded"), n(32, 32))

                def logits(s):
                    h, qb = STEPS_F[s]
                    w = (qb + 1) * P
                    e.wait_ge(sem("qk_product"), since("F", "qk_product", n(s + 1, NSF)))
                    if s >= 2:
                        e.wait_ge(sem("F_p_turned"), n(s - 1, NSF))
                    e.scalar_tensor_tensor(out=lg[s % 2][:, 0:w], in0=bank2(2 * (s % 2))[:, 0:w],
                                           scalar=c_q[:, qb, h:h + 1], in1=c_keys[h][:, 0:w],
                                           op0=ALU.add, op1=ALU.subtract).then_inc(sem("F_logits"), 1)
                    e.wait_ge(sem("F_logits"), n(s + 1, NSF))
                    ch(e.tensor_reduce(nmax[:, s:s + 1], lg[s % 2][:, 0:w], AX_X, ALU.max))
                    e.tensor_scalar(nmax[:, s:s + 1], nmax[:, s:s + 1], -1.0, None, ALU.mult)\
                        .then_inc(sem("F_row_max"), 1)

                for s in range(NSF):
                    logits(s)
                e.wait_ge(sem("weights_written"), since("F", "weights_written", n(NSF, NSF)))
                ch(e.reciprocal(den[:, :], den[:, :]))
                e.wait_ge(sem("F_p_turned"), n(NSF, NSF))
                e.tensor_copy(lg[0][:, :].rearrange("p (x d) -> p x d", d=HD),
                              den[:, :].rearrange("p (x o) -> p x o", o=1).to_broadcast([P, NSF, HD]))\
                    .then_inc(sem("F_den_spread"), 1)
                e.wait_ge(sem("F_den_taken"), n(1, 1))
                e.wait_ge(sem("weights_used"), since("F", "weights_used", n(NSF, NSF)))
                e.tensor_tensor(lg[1][:, :], lg[1][:, :], bank2(6), ALU.mult).then_inc(sem("F_o_divided"), 1)
                assert ch.n == K, ch.n
                e.wait_ge(sem("F_att_H"), n(1, 1))
                e.tensor_tensor(mixL[:, ds(0, 1), :].rearrange("p o t -> p (o t)"), lg[1][:, :],
                                f32(mixH[:, ds(0, 1), :].rearrange("p o t -> p (o t)")), ALU.subtract)\
                    .then_inc(sem("F_pair_done"), 1)
                e.wait_ge(sem("F_pair_done"), n(2, 1))

            pairs_F(e, pair)

        def pe_F(e):
            e.wait_ge(sem("block_L"), since("E", "block_L", NB))
            dense(e, UF, 0)
            e.wait_ge(sem("F_c_summed"), 1)
            for b in range(NB):
                mm = e.transpose(PS[:, 4, 8 * b:8 * b + 8], c_row[:, b * P:(b + 1) * P], ident[0:8, 0:8])
            mm.then_inc(sem("F_c_turned"), 1)
            e.wait_ge(sem("masks_written"), since("F", "masks_written", 1))
            e.wait_ge(sem("F_forget_taken"), 1)

            def pair(n, ds, u):
                blk = lambda b: slice(b * P, (b + 1) * P)

                def turn_to_tokens(src):
                    for b in range(NB):
                        mm = e.transpose(PS[:, 4 + b // 4, blk(b % 4)], src[:, blk(b)], ident[:, :])
                    return mm

                def unit(i):
                    if i >= 2:
                        e.wait_ge(sem("dense_tile_taken"), since("F", "dense_tile_taken", n(i - 1, 5)))
                    dense(e, unit_F(u, i)[0], 2 * (i % 2), *unit_F(u, i)[1:])

                unit(0)
                unit(1)
                e.wait_ge(sem("F_pair_done"), n(1, 1))
                e.wait_ge(sem("F_spatial_loaded"), n(48, 48))
                for g in range(2):
                    mm = e.transpose(PS[:, 6, blk(g)], wsp[:, g, :], ident[:, :])
                mm.then_inc(sem("F_spatial_turned"), 1)
                e.wait_ge(sem("norm_squares"), since("F", "norm_squares", n(1, 1)))
                for half in range(2):
                    mm = e.matmul(PS[:, 4 + half, :], same_F[:, :], lg[0][:, half * HALF:(half + 1) * HALF],
                                  start=True, stop=True)
                mm.then_inc(sem("norm_sums"), 1)
                unit(2)
                e.wait_ge(sem("F_vg_normalised"), n(1, 1))
                turn_to_tokens(vg_F).then_inc(sem("F_vg_turned"), 1)
                unit(3)
                e.wait_ge(sem("F_vg_tok"), n(1, 1))
                e.wait_ge(sem("F_spatial_masked"), n(1, 1))
                for g in range(2):
                    hs = slice(g * HD, (g + 1) * HD)
                    for b in range(NB):
                        mm = e.matmul(PS[hs, 6 + b // 4, blk(b % 4)], lg[1][:, b * P + g * HD:b * P + (g + 1) * HD],
                                      wspT[:, g, :], start=True, stop=True)
                mm.then_inc(sem("F_mixed"), 1)
                unit(4)
                e.wait_ge(sem("dense_tile_taken"), since("F", "dense_tile_taken", n(5, 5)))
                turn_to_tokens(v_F).then_inc(sem("v_att_turned"), 1)

                def qk(s):
                    h, qb = STEPS_F[s]
                    hs, bank, w = slice(h * HD, (h + 1) * HD), 2 * (s % 2), (qb + 1) * P
                    if s >= 2:
                        e.wait_ge(sem("F_logits"), n(s - 1, NSF))
                    for x0 in range(0, w, HALF):
                        x1 = min(w, x0 + HALF)
                        e.matmul(PS[:, bank + x0 // HALF, 0:x1 - x0], q_F[hs, blk(qb)], k_F[hs, x0:x1],
                                 start=True, stop=True)
                    e.matmul(PS[:, bank + (w - 1) // HALF, (qb % 4) * P:(qb % 4 + 1) * P], ident_F[:, :],
                             bar_F[:, :], start=False, stop=True, skip_group_check=True)\
                        .then_inc(sem("qk_product"), 1)

                def turn(s):
                    e.wait_ge(sem("weights_written"), since("F", "weights_written", n(s + 1, NSF)))
                    if s:
                        e.wait_ge(sem("F_p_taken"), n(s, NSF))
                    for b in range(STEPS_F[s][1] + 1):
                        mm = e.transpose(PS[:, 4 + b // 4, blk(b % 4)], lg[s % 2][:, blk(b)], ident[:, :])
                    mm.then_inc(sem("F_p_turned"), 1)

                def values(s):
                    h, qb = STEPS_F[s]
                    hs = slice(h * HD, (h + 1) * HD)
                    e.wait_ge(sem("F_p_taken"), n(s + 1, NSF))
                    for b in range(qb + 1):
                        mm = e.matmul(PS[hs, 6 + qb // 4, blk(qb % 4)], vt_F[:, b * P + h * HD:b * P + (h + 1) * HD],
                                      pT[s % 2][:, blk(b)], start=(b == 0), stop=(b == qb))
                    mm.then_inc(sem("weights_used"), 1)

                e.wait_ge(sem("F_gated"), n(1, 1))
                e.wait_ge(sem("v_att_tok"), since("F", "v_att_tok", n(1, 1)))
                qk(0)
                qk(1)
                for s in range(NSF):
                    turn(s)
                    if s + 2 < NSF:
                        qk(s + 2)
                    values(s)
                e.wait_ge(sem("F_den_spread"), n(1, 1))
                e.wait_ge(sem("F_p_taken"), n(NSF, NSF))
                turn_to_tokens(lg[0][:, :]).then_inc(sem("F_den_turned"), 1)

            pairs_F(e, pair)

        UG = UF + 1 + UPF * NPAIR
        UH = UG + 2 * KT

        def mixer_done(e):
            e.wait_ge(sem("F_pair_done"), NPAIR + 1)

        def sp_G(e):
            sp_rows(e, UG, w_out2)

        def pool_G(e):
            mixer_done(e)
            res_dma(e, "G", x2_scr, x3_scr, for_G)

        def act_G(e):
            mixer_done(e)
            act_rows(e, "G", UG, for_G, False)

        def dve_G(e):
            dve_rows(e, "G", UG, for_G, False, C_FPRE2)

        def pe_G(e):
            mixer_done(e)
            pe_rows(e, "G", UG, mixH, mixL)
            pe_turn(e, "G", for_G)

        def sp_H(e):
            sp_ffn(e, "H", "G", UH, w_up2, DFF, w_up2, 0, w_down2)
            load_unit(e, UH + 4 * NG, w_in[:, :, 0:P])
            for b in range(NB):
                e.wait_ge(sem("block_normalised"), since("H", "block_normalised", b + 1))
                e.dma_start(out_tok[:, b, :], yacc[:, b, :]).then_inc(sem("output_stored"), 16)
            e.wait_ge(sem("output_stored"), 16 * NB)

        def pool_H(e):
            ffn_memory_free(e, "G")
            res_dma(e, "H", x3_scr, None, for_E, a["norm_final_g_2"])

        def act_H(e):
            act_ffn(e, "H", "G", UH, True)
            for b in range(NB):
                act_x(e, "H", b, for_E)

        def dve_H(e):
            add = dve_ffn(e, "H", "G", UH, True)
            e.wait_ge(sem("gain_loaded"), since("H", "gain_loaded", 16))

            def final(b):
                e.wait_ge(sem("std2"), since("H", "std2", b + 1))
                e.reciprocal(rstd2[:, b:b + 1], sd2[:, b:b + 1]).then_inc(sem("rstd2"), 1)
                e.wait_ge(sem("rstd2"), since("H", "rstd2", b + 1))
                e.scalar_tensor_tensor(out=yacc[:, b, :], in0=x1E[b % 2][:, :], scalar=rstd2[:, b:b + 1],
                                       in1=gBE[:, :], op0=ALU.mult, op1=ALU.mult)\
                    .then_inc(sem("block_normalised"), 1)

            staged(add, lambda b: dve_x(e, "H", b, for_E, yacc, False, stored=False), final)

        def pe_H(e):
            staged(pe_ffn(e, "H", "G", UH, True))

        block = ctx.enter_context(nc.Block())

        @block.sync
        def _(e):
            sp_A(e)
            sp_B(e)
            sp_C(e)
            sp_D(e)
            sp_E(e)
            sp_F(e)
            sp_G(e)
            sp_H(e)

        @block.gpsimd
        def _(e):
            pool_A(e)
            pool_masks(e)
            pool_B(e)
            pool_D(e)
            pool_E(e)
            pool_F(e)
            pool_G(e)
            pool_H(e)

        @block.scalar
        def _(e):
            act_dma_A(e)
            act_A(e)
            act_B(e)
            act_C(e)
            act_D(e)
            act_E(e)
            act_F(e)
            act_G(e)
            act_H(e)

        @block.vector
        def _(e):
            dve_A(e)
            dve_B(e)
            dve_C(e)
            dve_D(e)
            dve_E(e)
            dve_F(e)
            dve_G(e)
            dve_H(e)

        @block.tensor
        def _(e):
            pe_A(e)
            pe_B(e)
            pe_C(e)
            pe_D(e)
            pe_E(e)
            pe_F(e)
            pe_G(e)
            pe_H(e)




def kernel(**inputs):
    import concourse.bacc as bacc
    from concourse.bass_utils import run_bass_kernel_spmd

    nc = bacc.Bacc("TRN2", target_bir_lowering=False, num_devices=1)
    arrays, aps = {}, {}
    for name, value in inputs.items():
        v = np.ascontiguousarray(value)
        arrays[f"in_{name}"] = v
        aps[name] = nc.dram_tensor(f"in_{name}", v.shape, F32, kind="ExternalInput").ap()
    out = nc.dram_tensor("out_0", [1, S, D], F32, kind="ExternalOutput").ap()
    build(nc, aps, out)
    r = run_bass_kernel_spmd(nc, [arrays], core_ids=[0])
    return r.results[0]["out_0"]
```
